# Optimizing a Trainium2 kernel written in Bass

```python
import math
import jax, jax.numpy as jnp
from jax import lax
import numpy as np

'''One inference step (2 trunk layers) of a hybrid chunk-causal streaming encoder.

Layer 0: token mixer A = DSA-style sparse attention (lightweight relu indexer, top-k key
selection, gathered GQA attention with ALiBi). Layer 1: token mixer B = differential attention
(Diff-Transformer) with ALiBi. Every layer: DeepNorm post-LN residual, then SwiGLU FFN plus a
sigmoid-gated per-layer input embedding, post-LN.

Inputs:
  x_prompt (BATCH, SEQ, D_MODEL), x_sample (DEC_BATCH, DEC_SEQ, D_MODEL)
  cache_a_k, cache_a_v (N_LAYERS_A, DEC_BATCH, PAST_LEN, A_KV_HEADS, A_HEAD_DIM)
  cache_a_kidx (N_LAYERS_A, DEC_BATCH, PAST_LEN, IDX_DIM)
  cache_b_k, cache_b_v (N_LAYERS_B, DEC_BATCH, PAST_LEN, B_HEADS, 2*B_HEAD_DIM)
  p_prompt (DEPTH, BATCH, SEQ, PLE_DIM), p_sample (DEPTH, DEC_BATCH, DEC_SEQ, PLE_DIM)
  weights (see setup_inputs)
Output tuple:
  y_prompt (BATCH, SEQ, D_MODEL), y_sample (DEC_BATCH, DEC_SEQ, D_MODEL),
  new_a_k_prompt, new_a_v_prompt (N_LAYERS_A, BATCH, SEQ, A_KV_HEADS, A_HEAD_DIM),
  new_a_kidx_prompt (N_LAYERS_A, BATCH, SEQ, IDX_DIM),
  new_b_k_prompt, new_b_v_prompt (N_LAYERS_B, BATCH, SEQ, B_HEADS, 2*B_HEAD_DIM),
  new_a_k_sample, new_a_v_sample (N_LAYERS_A, DEC_BATCH, DEC_SEQ, A_KV_HEADS, A_HEAD_DIM),
  new_a_kidx_sample (N_LAYERS_A, DEC_BATCH, DEC_SEQ, IDX_DIM),
  new_b_k_sample, new_b_v_sample (N_LAYERS_B, DEC_BATCH, DEC_SEQ, B_HEADS, 2*B_HEAD_DIM)
'''

D_MODEL = 1024
BATCH = 1
SEQ = 1024
DEPTH = 2
DEC_BATCH = 1
DEC_SEQ = 32
PAST_LEN = 128

CHUNK = 64
N_MIXERS = 2
N_LAYERS_A = (DEPTH + 1) // 2
N_LAYERS_B = DEPTH // 2

A_HEADS = 16
A_HEAD_DIM = D_MODEL // A_HEADS
A_KV_HEADS = 4
A_GROUP = A_HEADS // A_KV_HEADS
IDX_HEADS = 8
IDX_DIM = 64
TOPK_MAX = 256
A_QBLOCK = CHUNK
A_Q_COLS = A_HEADS * A_HEAD_DIM
A_KV_COLS = A_KV_HEADS * A_HEAD_DIM
IDX_Q_COLS = IDX_HEADS * IDX_DIM
A_SPLITS = (A_Q_COLS, A_Q_COLS + A_KV_COLS, A_Q_COLS + 2 * A_KV_COLS,
            A_Q_COLS + 2 * A_KV_COLS + IDX_Q_COLS, A_Q_COLS + 2 * A_KV_COLS + IDX_Q_COLS + IDX_DIM)
A_IN_COLS = A_SPLITS[-1] + IDX_HEADS
IDX_SCALE = IDX_DIM ** -0.5 * IDX_HEADS ** -0.5

B_HEADS = 8
B_HEAD_DIM = D_MODEL // (2 * B_HEADS)
B_QBLOCK = 128
B_IN_COLS = 3 * B_HEADS * 2 * B_HEAD_DIM

D_FF = -(-8 * D_MODEL // (3 * 256)) * 256
PLE_DIM = 256

ALPHA = (2 * DEPTH) ** 0.25
BETA = (8 * DEPTH) ** -0.25
LN_EPS = 1e-5

kernel_name = "dsa_diffattn_deepnorm_streaming_step"

def alibi_slopes(n_heads):
    return jnp.asarray(2.0 ** (-8.0 * np.arange(1, n_heads + 1) / n_heads), dtype=jnp.float32)

def chunk_limit(pos):
    return (pos // CHUNK + 1) * CHUNK

def layer_norm(x, g, b):
    xf = x.astype(jnp.float32)
    mu = jnp.mean(xf, axis=-1, keepdims=True)
    var = jnp.mean(jnp.square(xf - mu), axis=-1, keepdims=True)
    return ((xf - mu) * lax.rsqrt(var + LN_EPS) * g + b).astype(x.dtype)

def rms_norm(x, g):
    xf = x.astype(jnp.float32)
    return xf * lax.rsqrt(jnp.mean(jnp.square(xf), axis=-1, keepdims=True) + LN_EPS) * g

def dsa_project(x, w_in):
    B, T, _ = x.shape
    q, k, v, qi, ki, wi = jnp.split(x @ w_in, list(A_SPLITS), axis=-1)
    q = q.reshape(B, T, A_KV_HEADS, A_GROUP, A_HEAD_DIM)
    k = k.reshape(B, T, A_KV_HEADS, A_HEAD_DIM)
    v = v.reshape(B, T, A_KV_HEADS, A_HEAD_DIM)
    qi = qi.reshape(B, T, IDX_HEADS, IDX_DIM)
    return q, k, v, qi, ki, wi

def dsa_attend(q, qi, wi, q_pos, k, v, ki, n_sel):
    B, T = q.shape[:2]
    L = k.shape[1]
    key_pos = jnp.arange(L, dtype=jnp.int32)
    limit = chunk_limit(q_pos)
    admissible = key_pos[None, :] < limit[:, None]
    dots = jnp.einsum('bthd,bsd->bths', qi, ki, preferred_element_type=jnp.float32)
    score = jnp.einsum('bths,bth->bts', jax.nn.relu(dots), wi.astype(jnp.float32) * IDX_SCALE)
    score = jnp.where(admissible[None], score, -jnp.inf)
    _, sel = lax.top_k(score, n_sel)
    valid = sel < limit[None, :, None]
    gather = jax.vmap(lambda kb, ib: jnp.take(kb, ib, axis=0))
    k_sel = gather(k, sel)
    v_sel = gather(v, sel)
    logits = jnp.einsum('btcgd,btkcd->btcgk', q, k_sel,
                        preferred_element_type=jnp.float32) * (A_HEAD_DIM ** -0.5)
    dist = jnp.abs(q_pos[None, :, None] - sel).astype(jnp.float32)
    slopes = alibi_slopes(A_HEADS).reshape(A_KV_HEADS, A_GROUP)
    logits = logits - slopes[None, None, :, :, None] * dist[:, :, None, None, :]
    logits = jnp.where(valid[:, :, None, None, :], logits, -jnp.inf)
    probs = jax.nn.softmax(logits, axis=-1).astype(v.dtype)
    out = jnp.einsum('btcgk,btkcd->btcgd', probs, v_sel)
    return out.reshape(B, T, A_HEADS * A_HEAD_DIM)

def mixer_a_prompt(x, w_in, w_out, n_sel):
    B, S, _ = x.shape
    q, k, v, qi, ki, wi = dsa_project(x, w_in)
    nb = S // A_QBLOCK

    def to_blocks(t):
        return jnp.moveaxis(t.reshape(B, nb, A_QBLOCK, *t.shape[2:]), 1, 0)

    def body(args):
        qb, qib, wib, blk = args
        q_pos = blk * A_QBLOCK + jnp.arange(A_QBLOCK, dtype=jnp.int32)
        return dsa_attend(qb, qib, wib, q_pos, k, v, ki, n_sel)

    out = lax.map(body, (to_blocks(q), to_blocks(qi), to_blocks(wi), jnp.arange(nb, dtype=jnp.int32)))
    out = jnp.moveaxis(out, 0, 1).reshape(B, S, A_Q_COLS)
    return out @ w_out, k, v, ki

def mixer_a_sample(x, cache_k, cache_v, cache_ki, w_in, w_out, n_sel):
    B, T, _ = x.shape
    P = cache_k.shape[1]
    q, k, v, qi, ki, wi = dsa_project(x, w_in)
    k_all = jnp.concatenate([cache_k, k], axis=1)
    v_all = jnp.concatenate([cache_v, v], axis=1)
    ki_all = jnp.concatenate([cache_ki, ki], axis=1)
    q_pos = P + jnp.arange(T, dtype=jnp.int32)
    out = dsa_attend(q, qi, wi, q_pos, k_all, v_all, ki_all, n_sel)
    return out @ w_out, k, v, ki

def diff_project(x, w_in):
    B, T, _ = x.shape
    q, k, v = jnp.split(x @ w_in, 3, axis=-1)
    q = q.reshape(B, T, B_HEADS, 2, B_HEAD_DIM)
    k = k.reshape(B, T, B_HEADS, 2 * B_HEAD_DIM)
    v = v.reshape(B, T, B_HEADS, 2 * B_HEAD_DIM)
    return q, k, v

def diff_attend(q, q_pos, k, v, lam):
    B, L = k.shape[:2]
    k2 = k.reshape(B, L, B_HEADS, 2, B_HEAD_DIM)
    logits = jnp.einsum('bthmd,bshmd->bhmts', q, k2,
                        preferred_element_type=jnp.float32) * (B_HEAD_DIM ** -0.5)
    key_pos = jnp.arange(L, dtype=jnp.int32)
    dist = jnp.abs(q_pos[:, None] - key_pos[None, :]).astype(jnp.float32)
    slopes = alibi_slopes(B_HEADS)
    logits = logits - slopes[None, :, None, None, None] * dist
    admissible = key_pos[None, :] < chunk_limit(q_pos)[:, None]
    logits = jnp.where(admissible, logits, -jnp.inf)
    probs = jax.nn.softmax(logits, axis=-1)
    attn = probs[:, :, 0] - lam * probs[:, :, 1]
    return jnp.einsum('bhts,bshe->bthe', attn.astype(v.dtype), v)

def diff_lambda(lam_params, lambda_init):
    lp = lam_params.astype(jnp.float32)
    return jnp.exp(jnp.sum(lp[0] * lp[1])) - jnp.exp(jnp.sum(lp[2] * lp[3])) + lambda_init

def diff_finish(out, subln_g, w_out, lambda_init, dtype):
    B, T = out.shape[:2]
    o = rms_norm(out, subln_g) * (1.0 - lambda_init)
    return o.astype(dtype).reshape(B, T, B_HEADS * 2 * B_HEAD_DIM) @ w_out

def mixer_b_prompt(x, w_in, lam_params, subln_g, w_out, lambda_init):
    B, S, _ = x.shape
    q, k, v = diff_project(x, w_in)
    lam = diff_lambda(lam_params, lambda_init)
    nb = S // B_QBLOCK
    qb = jnp.moveaxis(q.reshape(B, nb, B_QBLOCK, B_HEADS, 2, B_HEAD_DIM), 1, 0)

    def body(args):
        qblk, blk = args
        q_pos = blk * B_QBLOCK + jnp.arange(B_QBLOCK, dtype=jnp.int32)
        return diff_attend(qblk, q_pos, k, v, lam)

    out = lax.map(body, (qb, jnp.arange(nb, dtype=jnp.int32)))
    out = jnp.moveaxis(out, 0, 1).reshape(B, S, B_HEADS, 2 * B_HEAD_DIM)
    return diff_finish(out, subln_g, w_out, lambda_init, x.dtype), k, v

def mixer_b_sample(x, cache_k, cache_v, w_in, lam_params, subln_g, w_out, lambda_init):
    B, T, _ = x.shape
    P = cache_k.shape[1]
    q, k, v = diff_project(x, w_in)
    lam = diff_lambda(lam_params, lambda_init)
    k_all = jnp.concatenate([cache_k, k], axis=1)
    v_all = jnp.concatenate([cache_v, v], axis=1)
    q_pos = P + jnp.arange(T, dtype=jnp.int32)
    out = diff_attend(q, q_pos, k_all, v_all, lam)
    return diff_finish(out, subln_g, w_out, lambda_init, x.dtype), k, v

def channel_and_ple(x, p, w13, w2, w_ple, w_gate, g, b):
    gate, up = jnp.split(x @ w13, 2, axis=-1)
    ffn = (jax.nn.silu(gate) * up) @ w2
    ple = jax.nn.sigmoid(x @ w_gate) * (p @ w_ple)
    return layer_norm(ALPHA * x + ffn + ple, g, b)

def setup_inputs(seed: int = 0) -> dict:
    key = jax.random.key(seed)
    ks = jax.random.split(key, 24)
    n = jax.random.normal
    f32 = jnp.float32
    return {
        'x_prompt': n(ks[0], (BATCH, SEQ, D_MODEL), f32),
        'x_sample': n(ks[1], (DEC_BATCH, DEC_SEQ, D_MODEL), f32),
        'cache_a_k': n(ks[2], (N_LAYERS_A, DEC_BATCH, PAST_LEN, A_KV_HEADS, A_HEAD_DIM), f32),
        'cache_a_v': n(ks[3], (N_LAYERS_A, DEC_BATCH, PAST_LEN, A_KV_HEADS, A_HEAD_DIM), f32),
        'cache_a_kidx': n(ks[4], (N_LAYERS_A, DEC_BATCH, PAST_LEN, IDX_DIM), f32),
        'cache_b_k': n(ks[5], (N_LAYERS_B, DEC_BATCH, PAST_LEN, B_HEADS, 2 * B_HEAD_DIM), f32),
        'cache_b_v': n(ks[6], (N_LAYERS_B, DEC_BATCH, PAST_LEN, B_HEADS, 2 * B_HEAD_DIM), f32),
        'p_prompt': n(ks[7], (DEPTH, BATCH, SEQ, PLE_DIM), f32),
        'p_sample': n(ks[8], (DEPTH, DEC_BATCH, DEC_SEQ, PLE_DIM), f32),
        'a_w_in': n(ks[9], (N_LAYERS_A, D_MODEL, A_IN_COLS), f32) * D_MODEL ** -0.5,
        'a_w_out': n(ks[10], (N_LAYERS_A, A_Q_COLS, D_MODEL), f32) * (A_Q_COLS ** -0.5 * BETA),
        'b_w_in': n(ks[11], (N_LAYERS_B, D_MODEL, B_IN_COLS), f32) * D_MODEL ** -0.5,
        'b_lambda': n(ks[12], (N_LAYERS_B, 4, B_HEAD_DIM), f32) * 0.1,
        'b_subln': 1.0 + 0.02 * n(ks[13], (N_LAYERS_B, 2 * B_HEAD_DIM), f32),
        'b_w_out': n(ks[14], (N_LAYERS_B, 2 * B_HEADS * B_HEAD_DIM, D_MODEL), f32) * ((2 * B_HEADS * B_HEAD_DIM) ** -0.5 * BETA),
        'ffn_w13': n(ks[15], (DEPTH, D_MODEL, 2 * D_FF), f32) * D_MODEL ** -0.5,
        'ffn_w2': n(ks[16], (DEPTH, D_FF, D_MODEL), f32) * (D_FF ** -0.5 * BETA),
        'ple_w_proj': n(ks[17], (DEPTH, PLE_DIM, D_MODEL), f32) * (PLE_DIM ** -0.5 * BETA),
        'ple_w_gate': n(ks[18], (DEPTH, D_MODEL, D_MODEL), f32) * D_MODEL ** -0.5,
        'ln_gain': 1.0 + 0.02 * n(ks[19], (DEPTH, 2, D_MODEL), f32),
        'ln_bias': 0.02 * n(ks[20], (DEPTH, 2, D_MODEL), f32),
    }

def reference(x_prompt, x_sample, cache_a_k, cache_a_v, cache_a_kidx, cache_b_k, cache_b_v,
              p_prompt, p_sample, a_w_in, a_w_out, b_w_in, b_lambda, b_subln, b_w_out,
              ffn_w13, ffn_w2, ple_w_proj, ple_w_gate, ln_gain, ln_bias):
    S = x_prompt.shape[1]
    L_sample = cache_a_k.shape[2] + x_sample.shape[1]
    n_sel_prompt = min(TOPK_MAX, S // 4)
    n_sel_sample = min(TOPK_MAX, L_sample // 4)

    yp, ys = x_prompt, x_sample
    a_k_p, a_v_p, a_ki_p, a_k_s, a_v_s, a_ki_s = [], [], [], [], [], []
    b_k_p, b_v_p, b_k_s, b_v_s = [], [], [], []
    for i in range(DEPTH):
        j = i // N_MIXERS
        if i % N_MIXERS == 0:
            mp, kp, vp, kip = mixer_a_prompt(yp, a_w_in[j], a_w_out[j], n_sel_prompt)
            ms, ksm, vsm, kism = mixer_a_sample(ys, cache_a_k[j], cache_a_v[j], cache_a_kidx[j],
                                                a_w_in[j], a_w_out[j], n_sel_sample)
            a_k_p.append(kp); a_v_p.append(vp); a_ki_p.append(kip)
            a_k_s.append(ksm); a_v_s.append(vsm); a_ki_s.append(kism)
        else:
            lambda_init = 0.8 - 0.6 * math.exp(-0.3 * i)
            mp, kp, vp = mixer_b_prompt(yp, b_w_in[j], b_lambda[j], b_subln[j], b_w_out[j], lambda_init)
            ms, ksm, vsm = mixer_b_sample(ys, cache_b_k[j], cache_b_v[j], b_w_in[j], b_lambda[j],
                                          b_subln[j], b_w_out[j], lambda_init)
            b_k_p.append(kp); b_v_p.append(vp)
            b_k_s.append(ksm); b_v_s.append(vsm)
        yp = layer_norm(ALPHA * yp + mp, ln_gain[i, 0], ln_bias[i, 0])
        ys = layer_norm(ALPHA * ys + ms, ln_gain[i, 0], ln_bias[i, 0])
        yp = channel_and_ple(yp, p_prompt[i], ffn_w13[i], ffn_w2[i], ple_w_proj[i], ple_w_gate[i],
                             ln_gain[i, 1], ln_bias[i, 1])
        ys = channel_and_ple(ys, p_sample[i], ffn_w13[i], ffn_w2[i], ple_w_proj[i], ple_w_gate[i],
                             ln_gain[i, 1], ln_bias[i, 1])

    new_a_k_prompt = jnp.stack(a_k_p)
    new_a_v_prompt = jnp.stack(a_v_p)
    new_a_kidx_prompt = jnp.stack(a_ki_p)
    new_b_k_prompt = jnp.stack(b_k_p)
    new_b_v_prompt = jnp.stack(b_v_p)
    new_a_k_sample = jnp.stack(a_k_s)
    new_a_v_sample = jnp.stack(a_v_s)
    new_a_kidx_sample = jnp.stack(a_ki_s)
    new_b_k_sample = jnp.stack(b_k_s)
    new_b_v_sample = jnp.stack(b_v_s)
    return (yp, ys, new_a_k_prompt, new_a_v_prompt, new_a_kidx_prompt, new_b_k_prompt, new_b_v_prompt,
            new_a_k_sample, new_a_v_sample, new_a_kidx_sample, new_b_k_sample, new_b_v_sample)


_drawn_inputs = setup_inputs


def setup_inputs(seed=0):
    import zlib

    import numpy as np

    out = dict(_drawn_inputs(seed))
    spreads = {}
    factors = {}
    for name, (base, spread) in spreads.items():
        noise = np.random.default_rng([zlib.crc32(name.encode()), seed]).standard_normal(out[name].shape)
        drawn = base * np.exp(spread * noise) if base else spread * noise
        out[name] = __import__('jax').numpy.asarray(drawn.astype(out[name].dtype))
    for name, factor in factors.items():
        out[name] = (out[name] * factor).astype(out[name].dtype)
    return out
```

```python
import math
from contextlib import ExitStack

import concourse.bass as bass
from concourse import mybir

ALU = mybir.AluOpType
ACT = mybir.ActivationFunctionType
F32 = mybir.dt.float32
F32R = mybir.dt.float32r

P = 128
D = 1024
KC = D // P
SEQ, NEW, PAST = 1024, 32, 128
TOK = SEQ + NEW
PIECES = 3
TP = TOK // PIECES
QT = SEQ // P
SAMPLE = QT
CHUNK = 64
KV = 4
IDXH, IDXD = 8, 64
TOPK, TOPK_SAMPLE = 256, (PAST + NEW) // 4
BH = 8
DFF = 2816
PLE = 256
DEPTH = 2
LIMIT = 99
ALPHA = (2 * DEPTH) ** 0.25
EPS = 1e-5
BIG = 1.0e30
BARRED = -3.0e38
TAKEN = -3.3e38
TAKEN_BELOW = -3.2e38
LOWEST = -3.4e38
IDX_SCALE = IDXD ** -0.5 * IDXH ** -0.5
LAMBDA_INIT = 0.8 - 0.6 * math.exp(-0.3)
A_IN = 2120
QI0, KI0 = 1536, 2048

KEYCOLS = TOK + PAST
VBLK = QT + 2
VNEW, VCACHE = QT, QT + 1


def keys_of(tile):
    return P * (tile + 1) if tile < QT else PAST + NEW


def bias_at(tile):
    return P * tile * (tile + 1) // 2


def first_query(tile):
    return P * tile if tile < QT else TOK - P


class Core:
    pass


def ring_plan():
    phases = [("index", 1, [0, 1, 0, 1, 0]), ("attnA", KV, [0, 1, 0]), ("outA", 4, [0, 1]),
              ("ple0", KC // 2, [0, 1, 2, 3]), ("ffn0", DFF // P // 2, [0, 1, 0, 1, 2, 3]),
              ("attnB", BH, [0, 1, 0]), ("outB", 4, [0, 1]),
              ("ple1", KC // 2, [0, 1, 2, 3]), ("ffn1", DFF // P // 2, [0, 1, 0, 1, 2, 3])]
    base, plan = [0] * 4, {}
    for name, passes, slots in phases:
        plan[name] = (tuple(base), slots)
        for s in range(4):
            base[s] += passes * slots.count(s)
    return plan


PLAN = ring_plan()


def turn(phase, i, u):
    base, slots = PLAN[phase]
    s = slots[u]
    return s, i * slots.count(s) + (base[s] + slots[:u].count(s))


def load_unit(c, sp, phase, i, u, parts, kc):
    s, n = turn(phase, i, u)
    sp.wait_ge(c.split[s], 2 * n + 2)
    for dst, src in parts:
        sp.dma_start(dst(c.w_raw[s][:, 0:kc]), src).then_inc(c.loaded[s], 32 // len(parts))


def whole(t):
    return t


def split_unit(c, pool, phase, i, u, kc):
    s, n = turn(phase, i, u)
    pool.wait_ge(c.loaded[s], 32 * n + 32)
    pool.wait_ge(c.used[s], n + 1)
    nc = c.nc
    zero = c.zeros[:, :].rearrange("p (a b) -> p a b", a=1).to_broadcast([P, kc, P])
    nc.gpsimd.tensor_tensor(c.w_hi[s][:, 0:kc], c.w_raw[s][:, 0:kc], zero, ALU.add).then_inc(c.split[s], 1)
    pool.wait_ge(c.split[s], 2 * n + 3)
    nc.gpsimd.tensor_tensor(c.w_lo[s][:, 0:kc], c.w_raw[s][:, 0:kc], c.w_hi[s][:, 0:kc].bitcast(F32),
                            ALU.subtract).then_inc(c.split[s], 1)


def unit_ready(c, pe, phase, i, u):
    s, n = turn(phase, i, u)
    pe.wait_ge(c.split[s], 2 * n + 4)
    return s


def piece_done(c, mm, t, sem, s):
    mm.then_inc(sem, 1) if t < PIECES - 1 else mm.then_inc(c.used[s], 1)


def await_piece(c, eng, phase, i, u, t, sem, before):
    if t < PIECES - 1:
        eng.wait_ge(sem, 2 * before + t + 1)
    else:
        s, n = turn(phase, i, u)
        eng.wait_ge(c.used[s], n + 2)


def product(c, out, terms):
    last, n = None, 0
    for (wh, wl), (xh, xl) in terms:
        for w, x in ((wh, xh), (wh, xl), (wl, xh)):
            last = c.nc.tensor.matmul(out, w, x, start=(n == 0), stop=(n == 3 * len(terms) - 1))
            n += 1
    return last


def unit_product(c, out, s, kc, xh, xl, t, cols=P):
    return product(c, out, [((c.w_hi[s][:, k, 0:cols], c.w_lo[s][:, k, 0:cols]),
                             (xh[:, k, piece(t)], xl[:, k, piece(t)])) for k in range(kc)])


def piece(t):
    return slice(TP * t, TP * t + TP)


def bank(c, b, n=512):
    return c.psum[:, 512 * b:512 * b + n]


def load_x(c):
    nc = c.nc
    nat = c.at("x_nat", [P, 2, D], F32, 0)
    par = c.at("ln_rows", [66, P], F32, 8192)
    lam = c.at("lam_rows", [P, 4 * 64], F32, 8704)
    lamp = c.at("lam_prod", [P, 64], F32, 9728)
    lsum = c.at("lam_sum", [P, 4], F32, 9984)
    s_nat = [c.sem("x_loaded0"), c.sem("x_loaded1")]
    s_tail, s_par = c.sem("x_sample_loaded"), c.sem("params_loaded")
    s_t, s_hi, s_lo = c.sem("x_transposed"), c.sem("x_hi_done"), c.sem("x_lo_done")
    s_c, s_l = c.sem("const_steps"), c.sem("lambda_steps")
    x = c.dram["x_prompt"].rearrange("b (t p) d -> (b t) p d", p=P)

    def sync(sp):
        sp.dma_start(nat[:, 0], x[0]).then_inc(s_nat[0], 16)
        sp.dma_start(nat[:, 1], x[1]).then_inc(s_nat[1], 16)
        sp.dma_start(par[0:32, :], c.dram["ln_gain"].rearrange("l w (k p) -> (l w k) p", p=P)).then_inc(s_par, 16)
        sp.dma_start(par[32:64, :], c.dram["ln_bias"].rearrange("l w (k p) -> (l w k) p", p=P)).then_inc(s_par, 16)
        sp.dma_start(par[64:65, :], c.dram["b_subln"]).then_inc(s_par, 16)
        sp.dma_start(par[65:66, :], c.dram["b_subln"]).then_inc(s_par, 16)
        sp.dma_start(lam[:, :], c.dram["b_lambda"].rearrange("l a d -> l (a d)").to_broadcast([P, 256])).then_inc(s_par, 16)
        with sp.Fori(0, 3) as i:
            for j in (0, 1):
                sp.wait_ge(s_t, 4 * i + 2 * j + 6)
                sp.dma_start(nat[:, j], c.x_rows[bass.ds(2 * P * i + P * (2 + j), P), :]).then_inc(s_nat[j], 16)
        sp.wait_ge(s_t, 4 + 4 * 3 + 2)
        sp.dma_start(nat[0:NEW, 0], c.dram["x_sample"].rearrange("b t d -> (b t) d")).then_inc(s_tail, 16)

    def pool(g):
        nc.gpsimd.memset(c.zeros[:, :], 0.0).then_inc(s_c, 1)
        nc.gpsimd.memset(c.ident[:, :], 0.0).then_inc(s_c, 1)
        nc.gpsimd.memset(c.mean_d[:, :], 1.0 / D).then_inc(s_c, 1)
        nc.gpsimd.memset(c.mean_p[:, :], 1.0 / P).then_inc(s_c, 1)
        nc.gpsimd.memset(c.eps[:, :], EPS).then_inc(s_c, 1)
        nc.gpsimd.memset(c.neg_one[:, :], -1.0).then_inc(s_c, 1)
        g.wait_ge(s_c, 6)
        nc.gpsimd.affine_select(out=c.ident[:, :], in_=c.ident[:, :], compare_op=ALU.not_equal, fill=1.0,
                                base=0, pattern=[[-1, P]], channel_multiplier=1).then_inc(s_c, 1)
        nc.gpsimd.iota(c.dist[:, :], pattern=[[-1, SEQ]], base=SEQ - P, channel_multiplier=1,
                       allow_small_or_imprecise_dtypes=True).then_inc(s_c, 1)
        for s in range(4):
            g.sem_inc(c.split[s], 2)

    def tensor(pe):
        for s in range(4):
            pe.sem_inc(c.used[s], 1)
        pe.sem_inc(s_t, 4)
        pe.wait_ge(s_c, 7)
        with pe.Fori(0, 4) as i:
            for j in (0, 1):
                pe.wait_ge(s_nat[j], 16 * i + 16)
                for b in (0, 1):
                    pe.wait_ge(s_lo, 4 * i + 2 * j + b + 1)
                    for k in range(4):
                        mm = nc.tensor.transpose(bank(c, 2 * j + b)[:, P * k:P * k + P],
                                                 nat[:, j, P * (4 * b + k):P * (4 * b + k) + P], c.ident[:, :])
                    mm.then_inc(s_t, 1)
        pe.wait_ge(s_tail, 16)
        for k in range(KC):
            mm = nc.tensor.transpose(bank(c, 4)[:, NEW * k:NEW * k + NEW], nat[0:NEW, 0, P * k:P * k + P],
                                     c.ident[0:NEW, 0:NEW])
        mm.then_inc(s_t, 1)
        pe.wait_ge(s_par, 80)
        nc.tensor.transpose(bank(c, 5)[:, 0:66], par[:, :], c.ident[0:66, 0:66]).then_inc(s_t, 1)

    def places(i, j):
        for b in (0, 1):
            yield 2 * j + b, (slice(4 * b, 4 * b + 4), bass.ds(2 * P * i + P * j, P)), b

    def scalar(act):
        with act.Fori(0, 4) as i:
            for j in (0, 1):
                for bk, (ks, ts), b in places(i, j):
                    act.wait_ge(s_t, 4 * i + 2 * j + b + 5)
                    nc.scalar.activation(c.x_hi[:, ks, ts], bank(c, bk).rearrange("p (k t) -> p k t", k=4),
                                         ACT.Copy).then_inc(s_hi, 1)
        act.wait_ge(s_t, 21)
        nc.scalar.activation(c.x_hi[:, :, SEQ:TOK], bank(c, 4, KC * NEW).rearrange("p (k t) -> p k t", k=KC),
                             ACT.Copy).then_inc(s_hi, 1)
        act.wait_ge(s_l, 2)
        nc.scalar.activation(lsum[:, 2:4], lsum[:, 0:2], ACT.Exp).then_inc(s_l, 1)

    def vector(v):
        v.sem_inc(s_lo, 4)
        for g2 in (0, 1):
            for m in (0, 1):
                sigma = 2.0 ** (-(2 * g2 + m + 1) / 2)
                nc.vector.memset(c.q_scale[64 * m:64 * m + 64, g2:g2 + 1], 0.125 / sigma)
                nc.vector.memset(c.neg_sigma[:, g2, m:m + 1], -sigma)
        with v.Fori(0, 4) as i:
            for j in (0, 1):
                for bk, (ks, ts), b in places(i, j):
                    v.wait_ge(s_hi, 4 * i + 2 * j + b + 1)
                    nc.vector.tensor_tensor(c.x_lo[:, ks, ts], bank(c, bk).rearrange("p (k t) -> p k t", k=4),
                                            c.x_hi[:, ks, ts].bitcast(F32), ALU.subtract).then_inc(s_lo, 1)
        v.wait_ge(s_hi, 17)
        nc.vector.tensor_tensor(c.x_lo[:, :, SEQ:TOK], bank(c, 4, KC * NEW).rearrange("p (k t) -> p k t", k=KC),
                                c.x_hi[:, :, SEQ:TOK].bitcast(F32), ALU.subtract).then_inc(s_lo, 1)
        v.wait_ge(s_t, 22)
        nc.vector.tensor_copy(c.params[:, :], bank(c, 5, 66)).then_inc(s_lo, 1)
        v.wait_ge(s_lo, 22)
        nc.vector.tensor_scalar(c.rms_gain[:, :], c.params[:, 64:65], 1.0 - LAMBDA_INIT, None,
                                ALU.mult).then_inc(s_lo, 1)
        v.wait_ge(s_c, 8)
        nc.vector.scalar_tensor_tensor(out=c.dist[:, :], in0=c.dist[:, :], scalar=-1.0, in1=c.dist[:, :],
                                       op0=ALU.mult, op1=ALU.max).then_inc(s_lo, 1)
        v.wait_ge(s_par, 80)
        for m in (0, 1):
            nc.vector.tensor_tensor_reduce(lamp[:, :], lam[:, P * m:P * m + 64], lam[:, P * m + 64:P * m + P],
                                           1.0, 0.0, ALU.mult, ALU.add, lsum[:, m:m + 1]).then_inc(s_l, 1)
            v.wait_ge(s_l, m + 1)
        v.wait_ge(s_l, 3)
        nc.vector.tensor_tensor(c.neg_lam[:, :], lsum[:, 3:4], lsum[:, 2:3], ALU.subtract).then_inc(s_l, 1)
        v.wait_ge(s_l, 4)
        nc.vector.tensor_scalar(c.neg_lam[:, :], c.neg_lam[:, :], -LAMBDA_INIT, None, ALU.add).then_inc(s_l, 1)

    return sync, pool, tensor, scalar, vector


def index_projection(c):
    nc = c.nc
    base = c.bias_bytes
    qi_hi = c.at("qi_hi", [P, 4, TOK], F32R, base)
    qi_lo = c.at("qi_lo", [P, 4, TOK], F32R, base + 16896)
    ki_hi = c.at("ki_hi", [P, KEYCOLS], F32R, base + 33792)
    ki_lo = c.at("ki_lo", [P, KEYCOLS], F32R, base + 38528)
    kw = c.at("kiw", [72, TOK], F32, base + 43264)
    kw_nat = c.at("kiw_nat", [P, 9, 72], F32, base + 47488)
    cache = c.at("kidx_cache", [P, IDXD], F32, base + 50080)
    c.qi, c.ki, c.kw_nat = (qi_hi, qi_lo), (ki_hi, ki_lo), kw_nat
    c.idx_free = base + 50336
    s_p, s_hi, s_lo = c.sem("idx_pieces"), c.sem("idx_hi_done"), c.sem("idx_lo_done")
    s_kw, s_nt, s_nat = c.sem("kiw_copied"), c.sem("kiw_transposed"), c.sem("kiw_nat_done")
    s_ca, s_out = c.sem("kidx_cache_loaded"), c.sem("kidx_stored")
    w = c.dram["a_w_in"][0].rearrange("(k p) n -> p k n", p=P)

    def sync(sp):
        for u in range(4):
            load_unit(c, sp, "index", 0, u, [(whole, w[:, :, QI0 + P * u:QI0 + P * u + P])], KC)
        load_unit(c, sp, "index", 0, 4, [(lambda t: t[:, :, 0:72], w[:, :, KI0:KI0 + 72])], KC)
        sp.wait_ge(c.phase_over, 3)
        sp.dma_start(cache[:, :], c.dram["cache_a_kidx"][0, 0]).then_inc(s_ca, 16)
        sp.wait_ge(s_nat, 2)
        sp.dma_start(c.dram["new_a_kidx_prompt"][0, 0].rearrange("(t p) d -> p t d", p=P),
                     kw_nat[:, 0:QT, 0:IDXD]).then_inc(s_out, 16)
        sp.dma_start(c.dram["new_a_kidx_sample"][0, 0], kw_nat[P - NEW:P, QT, 0:IDXD]).then_inc(s_out, 16)

    def pool(g):
        for u in range(5):
            split_unit(c, g, "index", 0, u, KC)

    def tensor(pe):
        for u in range(5):
            s = unit_ready(c, pe, "index", 0, u)
            for t in range(PIECES):
                b = 3 * (u % 2) + t
                if u >= 2:
                    pe.wait_ge(s_lo, 3 * (u - 2) + t + 1)
                last = unit_product(c, bank(c, b, TP) if u < 4 else c.psum[0:72, 512 * b:512 * b + TP], s, KC,
                                    c.x_hi, c.x_lo, t, P if u < 4 else 72)
                piece_done(c, last, t, s_p, s)
        pe.wait_ge(s_ca, 16)
        pe.wait_ge(s_lo, 12)
        nc.tensor.transpose(c.psum[0:64, 512 * 3:512 * 3 + P], cache[:, :], c.ident[:, :]).then_inc(s_nt, 1)
        pe.wait_ge(s_kw, 3)
        for t in range(9):
            b, at = (6, t) if t < 7 else (7, t - 7)
            q = first_query(t)
            mm = nc.tensor.transpose(bank(c, b)[:, 72 * at:72 * at + 72], kw[:, q:q + P], c.ident[0:72, 0:72])
            if t in (6, 8):
                mm.then_inc(s_nt, 1)

    def scalar(act):
        for u in range(4):
            for t in range(PIECES):
                await_piece(c, act, "index", 0, u, t, s_p, u)
                nc.scalar.activation(qi_hi[:, u, piece(t)], bank(c, 3 * (u % 2) + t, TP), ACT.Copy).then_inc(s_hi, 1)
        for t in range(PIECES):
            await_piece(c, act, "index", 0, 4, t, s_p, 4)
            src = c.psum[0:64, 512 * t:512 * t + TP]
            nc.scalar.activation(kw[:, piece(t)], c.psum[0:72, 512 * t:512 * t + TP], ACT.Copy).then_inc(s_kw, 1)
            nc.scalar.activation(ki_hi[0:64, piece(t)], src, ACT.Copy).then_inc(s_hi, 1)
            nc.scalar.activation(ki_hi[64:128, piece(t)], src, ACT.Copy).then_inc(s_hi, 1)
        act.wait_ge(s_nt, 1)
        for m in (0, 1):
            nc.scalar.activation(ki_hi[64 * m:64 * m + 64, TOK:KEYCOLS], c.psum[0:64, 512 * 3:512 * 3 + P],
                                 ACT.Copy).then_inc(s_hi, 1)

    def vector(v):
        for u in range(4):
            for t in range(PIECES):
                v.wait_ge(s_hi, 3 * u + t + 1)
                nc.vector.tensor_tensor(qi_lo[:, u, piece(t)], bank(c, 3 * (u % 2) + t, TP),
                                        qi_hi[:, u, piece(t)].bitcast(F32), ALU.subtract).then_inc(s_lo, 1)
        for t in range(PIECES):
            v.wait_ge(s_hi, 12 + 2 * t + 2)
            for m in (0, 1):
                nc.vector.tensor_tensor(ki_lo[64 * m:64 * m + 64, piece(t)], c.psum[0:64, 512 * t:512 * t + TP],
                                        ki_hi[0:64, piece(t)].bitcast(F32), ALU.subtract).then_inc(s_lo, 1)
        v.wait_ge(s_hi, 20)
        for m in (0, 1):
            nc.vector.tensor_tensor(ki_lo[64 * m:64 * m + 64, TOK:KEYCOLS], c.psum[0:64, 512 * 3:512 * 3 + P],
                                    ki_hi[0:64, TOK:KEYCOLS].bitcast(F32), ALU.subtract).then_inc(s_lo, 1)
        v.wait_ge(s_nt, 3)
        nc.vector.tensor_copy(kw_nat[:, 0:7, :], bank(c, 6, 504).rearrange("p (t n) -> p t n", n=72)).then_inc(s_nat, 1)
        nc.vector.tensor_copy(kw_nat[:, 7:9, :], bank(c, 7, 144).rearrange("p (t n) -> p t n", n=72)).then_inc(s_nat, 1)
        v.wait_ge(s_nat, 2)
        nc.vector.tensor_scalar(c.idx_w[:, :, :], kw_nat[:, :, 64:72], IDX_SCALE, None, ALU.mult).then_inc(s_nat, 1)

    c.kidx_stored = lambda eng: eng.wait_ge(s_out, 32)
    return sync, pool, tensor, scalar, vector


def selection(c):
    nc = c.nc
    relu = [c.at(f"relu{j}", [P, SEQ], F32, c.idx_free + 4096 * j) for j in (0, 1)]
    top8 = c.at("top8", [P, 8], F32, c.idx_free + 8192)
    s_dot, s_relu, s_acc, s_top = c.sem("dots"), c.sem("relu_done"), c.sem("scores_added"), c.sem("top_steps")
    ranked = list(range(2, QT)) + [SAMPLE]
    work = [(t, h) for t in ranked for h in range(IDXH)]

    def dist_of(t, n):
        at = P * (QT - 1 - t) if t < QT else (SEQ - P) - 32
        return c.dist[:, at:at + n]

    def tensor(pe):
        for n, (t, h) in enumerate(work):
            L, q, ch, m = keys_of(t), first_query(t), h // 2, h % 2
            if n >= 4:
                pe.wait_ge(s_relu, n - 3)
            rows = slice(64 * m, 64 * m + 64)
            parts = [(0, P, TOK), (P, NEW, SEQ)] if t == SAMPLE else [(a, min(512, L - a), a) for a in range(0, L, 512)]
            for at, w, key in parts:
                o = c.psum[:, 1024 * (n % 4) + at:1024 * (n % 4) + at + w]
                last = product(c, o, [((c.qi[0][rows, ch, q:q + P], c.qi[1][rows, ch, q:q + P]),
                                       (c.ki[0][rows, key:key + w], c.ki[1][rows, key:key + w]))])
            last.then_inc(s_dot, 1)

    def scalar(act):
        for n, (t, h) in enumerate(work):
            L = keys_of(t)
            act.wait_ge(s_dot, n + 1)
            if n >= 2:
                act.wait_ge(s_acc, n - 1)
            nc.scalar.activation(relu[n % 2][:, 0:L], c.psum[:, 1024 * (n % 4):1024 * (n % 4) + L],
                                 ACT.Relu).then_inc(s_relu, 1)

    def vector(v):
        for t in (0, 1):
            L = keys_of(t)
            o = c.bias[:, bias_at(t):bias_at(t) + L]
            nc.vector.tensor_copy(o, dist_of(t, L)).then_inc(s_top, 1)
        v.wait_ge(s_top, 2)
        for t in (0, 1):
            e = bias_at(t) + keys_of(t)
            nc.vector.memset(c.bias[0:64, e - CHUNK:e], BIG).then_inc(s_top, 1)
        step = 4
        for n, (t, h) in enumerate(work):
            L = keys_of(t)
            score = c.bias[:, bias_at(t):bias_at(t) + L]
            v.wait_ge(s_relu, n + 1)
            weight = c.idx_w[:, t, h:h + 1]
            if h == 0:
                nc.vector.tensor_scalar(score, relu[n % 2][:, 0:L], weight, None, ALU.mult).then_inc(s_acc, 1)
            else:
                v.wait_ge(s_acc, n)
                nc.vector.scalar_tensor_tensor(out=score, in0=relu[n % 2][:, 0:L], scalar=weight, in1=score,
                                               op0=ALU.mult, op1=ALU.add).then_inc(s_acc, 1)
        for t in ranked:
            L = keys_of(t)
            score = c.bias[:, bias_at(t):bias_at(t) + L]
            v.wait_ge(s_acc, len(work))
            if t < QT:
                nc.vector.memset(c.bias[0:64, bias_at(t) + L - CHUNK:bias_at(t) + L], BARRED).then_inc(s_top, 1)
                step += 1
            v.wait_ge(s_top, step)
            rounds = (TOPK if t < QT else TOPK_SAMPLE) // 8
            for r in range(rounds):
                v.wait_ge(s_top, step + 2 * r)
                nc.vector.max(top8[:, :], score).then_inc(s_top, 1)
                v.wait_ge(s_top, step + 2 * r + 1)
                nc.vector.match_replace(score, top8[:, :], score, TAKEN).then_inc(s_top, 1)
            step += 2 * rounds
            v.wait_ge(s_top, step)
            nc.vector.tensor_scalar(score, score, TAKEN_BELOW, BIG, ALU.is_ge, ALU.mult).then_inc(s_top, 1)
            step += 1
            v.wait_ge(s_top, step)
            nc.vector.tensor_tensor(score, score, dist_of(t, L), ALU.add).then_inc(s_top, 1)
            step += 1
        v.wait_ge(s_top, step)

    return None, None, tensor, scalar, vector, c.kidx_stored


def attention(c, kind):
    nc = c.nc
    A = kind == "A"
    name = "attn" + kind
    passes = KV if A else BH
    steps = [(g2, t) for g2 in ((0, 1) if A else (0,)) for t in range(QT + 1)]
    N = len(steps)
    no = c.phase_no
    at = c.bias_bytes if A else 0
    def place(nm, shape, dt, size=None):
        nonlocal at
        t = c.at(nm + kind, shape, dt, at)
        n = 4
        for x in shape[1:]:
            n *= x
        at += -(-n // 32) * 32
        return t
    q_hi, q_lo = place("q_hi", [P, TOK], F32R), place("q_lo", [P, TOK], F32R)
    k_hi, k_lo = place("k_hi", [P, KEYCOLS], F32R), place("k_lo", [P, KEYCOLS], F32R)
    v_hi, v_lo = place("v_hi", [P, VBLK, P], F32R), place("v_lo", [P, VBLK, P], F32R)
    slots = 2 if A else 3
    pt_hi, pt_lo = place("pt_hi", [P, slots, 512], F32R), place("pt_lo", [P, slots, 512], F32R)
    kc_nat = place("k_cache", [P, P], F32)
    vc_nat = kc_nat if A else place("v_cache", [P, P], F32)
    v_nat = None if A else place("v_nat", [P, 9, P], F32)
    if not A:
        dist = place("dist", [P, SEQ + PAST + NEW], F32)
    stat = place("stat", [P, 3, 10], F32)
    p_at = at
    prob = place("prob", [P, 3, 2, SEQ], F32)
    k_col = c.at("k_col" + kind, [P, TOK], F32, p_at)
    v_col = k_col if A else c.at("v_colB", [P, TOK], F32, p_at + 8192)
    k_nat = c.at("k_nat" + kind, [P, 9, P], F32, p_at + 16384)
    assert c.base + at <= c.end, (c.base + at, c.end)

    S = lambda n: c.sem(n + kind)
    s_piece, s_phi, s_plo = S("pieces"), S("pieces_hi"), S("pieces_lo")
    s_nt, s_nhi, s_nlo = S("rows_transposed"), S("rows_hi"), S("rows_done")
    s_cache, s_out = S("cache_loaded"), S("rows_stored")
    s_s, s_t, s_nb, s_exp, s_norm = S("logits"), S("logits_read"), S("row_max"), S("exp_done"), S("probs_ready")
    s_small, s_cleared = S("small_steps"), S("max_cleared")
    s_pt, s_pthi, s_ptlo = S("probs_transposed"), S("probsT_hi"), S("probsT_lo")
    s_o, s_oe = S("outputs"), S("outputs_read")
    s_dist, s_iota = S("dist_scaled"), S("dist_counted")

    per = 2 if A else 4
    def blocks(t):
        return list(range(t + 1)) if t < QT else [VCACHE, VNEW]
    def groups(t):
        b = blocks(t)
        return [b[j:j + per] for j in range(0, len(b), per)]
    first_group, g = [], 0
    for _, t in steps:
        first_group.append(g)
        g += len(groups(t))
    GROUPS = g
    wd = 64 if A else P

    def columns(a, at):
        return a[0, 0].rearrange("s h d -> s (h d)")[:, bass.ds(at, wd)]

    LOS = 9 if A else 6
    unit_banks = [[0, 1, 2], [3, 6, 7], [0, 1, 2]]
    ROWGROUPS = 3 if A else 6
    w = (c.dram["a_w_in"] if A else c.dram["b_w_in"])[0].rearrange("(k p) n -> p k n", p=P)

    def sync(sp):
        def weights(start, width, at):
            return w[:, :, start:][:, :, bass.ds(at, width)]

        with sp.Fori(0, passes) as i:
            head, pair = sp.snap(i * wd), sp.snap(i * 2 * P)
            if A:
                load_unit(c, sp, name, i, 0, [(lambda x: x[:, :, 0:64], weights(1024, 64, head)),
                                              (lambda x: x[:, :, 64:128], weights(1280, 64, head))], KC)
                load_unit(c, sp, name, i, 1, [(whole, weights(0, P, pair))], KC)
            else:
                load_unit(c, sp, name, i, 0, [(whole, weights(0, P, head))], KC)
                load_unit(c, sp, name, i, 1, [(whole, weights(D, P, head))], KC)
            load_unit(c, sp, name, i, 2, [(whole, weights(P, P, pair) if A else weights(2 * D, P, head))], KC)
        sp.wait_ge(s_out, 64 * passes)

    def pool(g):
        if not A:
            g.wait_ge(c.phase_over, 3 * no)
            nc.gpsimd.iota(dist[:, 0:SEQ], pattern=[[-1, SEQ]], base=SEQ - P, channel_multiplier=1,
                           allow_small_or_imprecise_dtypes=True).then_inc(s_iota, 1)
            nc.gpsimd.iota(dist[:, SEQ:], pattern=[[-1, PAST + NEW]], base=NEW, channel_multiplier=1,
                           allow_small_or_imprecise_dtypes=True).then_inc(s_iota, 1)
        with g.Fori(0, passes) as i:
            for u in range(3):
                split_unit(c, g, name, i, u, KC)

    def tensor(pe):
        def unit(i, u):
            s = unit_ready(c, pe, name, i, u)
            for t in range(PIECES):
                o = bank(c, unit_banks[u][t], TP)
                last = unit_product(c, o, s, KC, c.x_hi, c.x_lo, t)
                piece_done(c, last, t, s_piece, s)

        def row_group(i, n, src, tiles, extra=None):
            b = bank(c, 4 + n % 2)
            if n >= 2:
                pe.wait_ge(s_nlo, (ROWGROUPS + 1) * i + n + 1)
            for j, t in enumerate(tiles):
                cols = P if t < QT else NEW
                mm = nc.tensor.transpose(b[0:cols, P * j:P * j + P], src[:, P * t:P * t + cols], c.ident[:, :])
            if extra is not None:
                mm = nc.tensor.transpose(b[:, P:2 * P], extra[:, :], c.ident[:, :])
            mm.then_inc(s_nt, 1)

        def logits(i, s):
            g2, t = steps[s]
            L, q = keys_of(t), first_query(t)
            parts = [(0, P, TOK), (P, NEW, SEQ)] if t == SAMPLE else [(a, min(512, L - a), a) for a in range(0, L, 512)]
            for m in (0, 1):
                if s > 0:
                    pe.wait_ge(s_t, i * 2 * N + 2 * (s - 1) + m + 1 + 1)
                rows = slice(64 * m, 64 * m + 64)
                for a, n, key in parts:
                    o = c.psum[:, 1024 * m + a:1024 * m + a + n]
                    last = product(c, o, [((q_hi[rows, q:q + P], q_lo[rows, q:q + P]),
                                           (k_hi[rows, key:key + n], k_lo[rows, key:key + n]))])
                last.then_inc(s_s, 1)

        def output(i, s):
            g2, t = steps[s]
            gs, ob = groups(t), bank(c, 6 + s % 2)
            pe.wait_ge(s_norm, i * N + s + 1)
            pr = prob[:, s % 3]

            def turn_over(j):
                n = first_group[s] + j
                if n >= 2:
                    pe.wait_ge(s_ptlo, i * GROUPS + n - 2 + 1 + 1)
                b = bank(c, 4 + n % 2)
                for x, blk in enumerate(gs[j]):
                    key = P * (per * j + x)
                    w_ = NEW if blk == VNEW else P
                    for m in range(2 if A else 1):
                        col = P * ((2 * x + m) if A else x)
                        mm = nc.tensor.transpose(b[0:w_, col:col + P], pr[:, m, key:key + w_], c.ident[:, :])
                mm.then_inc(s_pt, 1)

            def multiply(j):
                n = first_group[s] + j
                pe.wait_ge(s_ptlo, i * GROUPS + n + 1 + 1)
                sl = n % slots
                width = 2 * P if A else P
                for x, blk in enumerate(gs[j]):
                    r = slice(0, NEW if blk == VNEW else P)
                    cols = slice(width * x, width * x + width)
                    first, lastb = (j == 0 and x == 0), (j == len(gs) - 1 and x == len(gs[j]) - 1)
                    trio = ((v_hi, pt_hi), (v_hi, pt_lo), (v_lo, pt_hi))
                    for k, (vv, pp) in enumerate(trio):
                        mm = nc.tensor.matmul(ob[:, 0:width], vv[r, blk, :], pp[r, sl, cols],
                                              start=(first and k == 0), stop=(lastb and k == 2))
                return mm

            turn_over(0)
            for j in range(len(gs)):
                if j + 1 < len(gs):
                    turn_over(j + 1)
                if j == 0 and s >= 2:
                    pe.wait_ge(s_oe, i * N + s - 2 + 1 + 1)
                mm = multiply(j)
            mm.then_inc(s_o, 1)

        with pe.Fori(0, passes) as i:
            pe.wait_ge(s_t, i * 2 * N + 1)
            unit(i, 0)
            pe.wait_ge(s_oe, i * N + 1)
            unit(i, 1)
            pe.wait_ge(s_ptlo, i * GROUPS + 1)
            if A:
                pe.wait_ge(s_cache, 32 * i + 32)
                pe.wait_ge(s_phi, 9 * i + 3)
                row_group(i, 0, k_col, range(0, 4))
                row_group(i, 1, k_col, range(4, 8))
                row_group(i, 2, k_col, [QT], kc_nat)
            else:
                pe.wait_ge(s_plo, LOS * i + 3)
                unit(i, 2)
                pe.wait_ge(s_cache, 32 * i + 32)
                pe.wait_ge(s_phi, 9 * i + 6)
                row_group(i, 0, k_col, range(0, 4))
                row_group(i, 1, k_col, range(4, 8))
                row_group(i, 2, k_col, [QT], kc_nat)
                pe.wait_ge(s_phi, 9 * i + 9)
                row_group(i, 3, v_col, range(0, 4))
                row_group(i, 4, v_col, range(4, 8))
                row_group(i, 5, v_col, [QT])
            pe.wait_ge(s_plo, LOS * i + 6)
            pe.wait_ge(s_nlo, (ROWGROUPS + 1) * i + ROWGROUPS + 1 + 1)
            for s in range(N):
                if A and s == QT + 1:
                    pe.wait_ge(s_t, i * 2 * N + 2 * s + 1)
                    unit(i, 2)
                    pe.wait_ge(s_plo, LOS * i + 9)
                logits(i, s)
                if s >= 2:
                    output(i, s - 2)
            output(i, N - 2)
            output(i, N - 1)

    def scalar(act):
        def q_piece(i, n, t, u, g2):
            await_piece(c, act, name, i, u, t, s_piece, 3 * i + u)
            nc.scalar.activation(q_hi[:, piece(t)], bank(c, unit_banks[u][t], TP), ACT.Copy,
                                 scale=c.q_scale[:, g2:g2 + 1] if A else 0.125).then_inc(s_phi, 1)

        def exps(i, s):
            g2, t = steps[s]
            L = keys_of(t)
            act.wait_ge(s_nb, i * N + s + 1)
            for m in (0, 1):
                sigma = 2.0 ** (-(2 * g2 + m + 1) / 2) if A else 1.0
                nc.scalar.activation(prob[:, s % 3, m, 0:L], prob[:, s % 3, m, 0:L], ACT.Exp,
                                     bias=stat[:, s % 3, 2 + m:3 + m], scale=sigma,
                                     accum_out=stat[:, s % 3, 4 + m:5 + m]).then_inc(s_exp, 1)

        def transposed(i, s):
            g2, t = steps[s]
            for j, gr in enumerate(groups(t)):
                n = first_group[s] + j
                act.wait_ge(s_pt, i * GROUPS + n + 1)
                width = (2 * P if A else P)
                sl, b = n % slots, bank(c, 4 + n % 2)
                if t == SAMPLE:
                    nc.scalar.activation(pt_hi[:, sl, 0:width], b[:, 0:width], ACT.Copy).then_inc(s_pthi, 1)
                    nc.scalar.activation(pt_hi[0:NEW, sl, width:2 * width], b[0:NEW, width:2 * width],
                                         ACT.Copy).then_inc(s_pthi, 1)
                else:
                    e = width * len(gr)
                    nc.scalar.activation(pt_hi[:, sl, 0:e], b[:, 0:e], ACT.Copy).then_inc(s_pthi, 2)

        with act.Fori(0, passes) as i:
            head = act.snap(i * wd)
            act.wait_ge(s_nlo, (ROWGROUPS + 1) * i + 1)
            if A:
                act.dma_start(kc_nat[:, 0:64], columns(c.dram["cache_a_k"], head)).then_inc(s_cache, 16)
                act.dma_start(kc_nat[:, 64:128], columns(c.dram["cache_a_v"], head)).then_inc(s_cache, 16)
            else:
                act.dma_start(kc_nat[:, :], columns(c.dram["cache_b_k"], head)).then_inc(s_cache, 16)
                act.dma_start(vc_nat[:, :], columns(c.dram["cache_b_v"], head)).then_inc(s_cache, 16)
            if A:
                for t in range(PIECES):
                    await_piece(c, act, name, i, 0, t, s_piece, 3 * i)
                    b = unit_banks[0][t]
                    nc.scalar.activation(k_col[:, piece(t)], bank(c, b, TP), ACT.Copy)
                    src = c.psum[0:64, 512 * b:512 * b + TP]
                    nc.scalar.activation(k_hi[0:64, piece(t)], src, ACT.Copy)
                    nc.scalar.activation(k_hi[64:128, piece(t)], src, ACT.Copy).then_inc(s_phi, 1)
                for t in range(PIECES):
                    q_piece(i, 3 + t, t, 1, 0)
            else:
                for t in range(PIECES):
                    q_piece(i, t, t, 0, 0)
                for t in range(PIECES):
                    await_piece(c, act, name, i, 1, t, s_piece, 3 * i + 1)
                    nc.scalar.activation(k_col[:, piece(t)], bank(c, unit_banks[1][t], TP), ACT.Copy)
                    nc.scalar.activation(k_hi[:, piece(t)], bank(c, unit_banks[1][t], TP), ACT.Copy).then_inc(s_phi, 1)
                for t in range(PIECES):
                    await_piece(c, act, name, i, 2, t, s_piece, 3 * i + 2)
                    nc.scalar.activation(v_col[:, piece(t)], bank(c, unit_banks[2][t], TP), ACT.Copy).then_inc(s_phi, 1)
            act.wait_ge(s_cache, 32 * i + 32)
            act.wait_ge(s_nt, ROWGROUPS * i + 1)
            nc.scalar.activation(v_hi[:, VCACHE, :], vc_nat[:, :], ACT.Copy).then_inc(s_nhi, 1)
            for n in range(ROWGROUPS):
                b = bank(c, 4 + n % 2)
                act.wait_ge(s_nt, ROWGROUPS * i + n + 1)
                if n == 2:
                    if A:
                        nc.scalar.activation(k_hi[0:64, TOK:KEYCOLS], b[0:64, P:2 * P], ACT.Copy)
                        ins = nc.scalar.activation(k_hi[64:128, TOK:KEYCOLS], b[0:64, P:2 * P], ACT.Copy)
                    else:
                        ins = nc.scalar.activation(k_hi[:, TOK:KEYCOLS], b[:, P:2 * P], ACT.Copy)
                if A or n >= 3:
                    r = n % 3
                    if r < 2:
                        ins = nc.scalar.activation(v_hi[:, 4 * r:4 * r + 4, :], b.rearrange("p (t d) -> p t d", t=4), ACT.Copy)
                    else:
                        ins = nc.scalar.activation(v_hi[0:NEW, VNEW, :], b[0:NEW, 0:P], ACT.Copy)
                if A or n >= 2:
                    ins.then_inc(s_nhi, 1)
            act.wait_ge(s_nlo, (ROWGROUPS + 1) * i + ROWGROUPS + 2)
            if A:
                outs = [(c.dram["new_a_k_prompt"], c.dram["new_a_k_sample"], k_nat, 0), (c.dram["new_a_v_prompt"], c.dram["new_a_v_sample"], k_nat, 64)]
            else:
                outs = [(c.dram["new_b_k_prompt"], c.dram["new_b_k_sample"], k_nat, 0), (c.dram["new_b_v_prompt"], c.dram["new_b_v_sample"], v_nat, 0)]
            for big, small, rows, o in outs:
                act.dma_start(big[0, 0].rearrange("(t p) h d -> p t (h d)", p=P)[:, :, bass.ds(head, wd)],
                             rows[:, 0:QT, o:o + wd]).then_inc(s_out, 16)
                act.dma_start(columns(small, head),
                             rows[0:NEW, QT, o:o + wd]).then_inc(s_out, 16)
            for s in range(N + 2):
                if 1 <= s <= N:
                    exps(i, s - 1)
                if A and s == QT + 1:
                    for t in range(PIECES):
                        q_piece(i, 6 + t, t, 2, 1)
                if s >= 2:
                    transposed(i, s - 2)

    HI_ROWS = 4 if A else 5

    def vector(v):
        def q_piece(i, n, t, u, g2):
            v.wait_ge(s_phi, 9 * i + n + 1)
            nc.vector.scalar_tensor_tensor(out=q_lo[:, piece(t)], in0=bank(c, unit_banks[u][t], TP),
                                           scalar=c.q_scale[:, g2:g2 + 1] if A else 0.125,
                                           in1=q_hi[:, piece(t)].bitcast(F32), op0=ALU.mult,
                                           op1=ALU.subtract).then_inc(s_plo, 1)

        def read_logits(i, s):
            g2, t = steps[s]
            L, sl = keys_of(t), s % 3
            for m in (0, 1):
                v.wait_ge(s_s, i * 2 * N + 2 * s + m + 1)
                if s == 2 and m == 0:
                    v.wait_ge(s_out, 64 * i + 64)
                if A:
                    b = c.bias[:, bias_at(t):bias_at(t) + L]
                else:
                    o = P * (QT - 1 - t) if t < QT else SEQ
                    b = dist[:, o:o + L]
                nc.vector.memset(stat[:, sl, 8 + m:9 + m], 0.0).then_inc(s_cleared, 1)
                nc.vector.tensor_tensor_reduce(prob[:, sl, m, 0:L], c.psum[:, 1024 * m:1024 * m + L], b, 1.0,
                                               LOWEST, ALU.subtract, ALU.max,
                                               stat[:, sl, m:m + 1]).then_inc(s_t, 1)
            v.wait_ge(s_t, i * 2 * N + 2 * s + 2 + 1)
            neg = c.neg_sigma[:, g2, :] if A else c.neg_one[:, :]
            nc.vector.tensor_tensor(stat[:, sl, 2:4], stat[:, sl, 0:2], neg, ALU.mult).then_inc(s_nb, 1)

        def normalise(i, s):
            g2, t = steps[s]
            L, sl = keys_of(t), s % 3
            v.wait_ge(s_exp, i * 2 * N + 2 * s + 2)
            nc.vector.reciprocal(stat[:, sl, 6:8], stat[:, sl, 4:6]).then_inc(s_small, 1)
            v.wait_ge(s_small, (i * N + s) * (1 if A else 3) + 1)
            p0, p1 = prob[:, sl, 0, 0:L], prob[:, sl, 1, 0:L]
            if A:
                nc.vector.tensor_scalar(p0, p0, stat[:, sl, 6:7], None, ALU.mult)
                nc.vector.tensor_scalar(p1, p1, stat[:, sl, 7:8], None, ALU.mult).then_inc(s_norm, 1)
            else:
                nc.vector.tensor_tensor(stat[:, sl, 7:8], stat[:, sl, 7:8], c.neg_lam[:, :], ALU.mult).then_inc(s_small, 1)
                v.wait_ge(s_small, (i * N + s) * 3 + 2)
                nc.vector.tensor_scalar(p1, p1, stat[:, sl, 7:8], None, ALU.mult).then_inc(s_small, 1)
                v.wait_ge(s_small, (i * N + s) * 3 + 3)
                nc.vector.scalar_tensor_tensor(out=p0, in0=p0, scalar=stat[:, sl, 6:7], in1=p1, op0=ALU.mult,
                                               op1=ALU.add).then_inc(s_norm, 1)

        def transposed(i, s):
            g2, t = steps[s]
            for j, gr in enumerate(groups(t)):
                n = first_group[s] + j
                v.wait_ge(s_pthi, 2 * (i * GROUPS + n + 1))
                width = (2 * P if A else P)
                sl, b = n % slots, bank(c, 4 + n % 2)
                if t == SAMPLE:
                    nc.vector.tensor_tensor(pt_lo[:, sl, 0:width], b[:, 0:width],
                                            pt_hi[:, sl, 0:width].bitcast(F32), ALU.subtract)
                    nc.vector.tensor_tensor(pt_lo[0:NEW, sl, width:2 * width], b[0:NEW, width:2 * width],
                                            pt_hi[0:NEW, sl, width:2 * width].bitcast(F32),
                                            ALU.subtract).then_inc(s_ptlo, 1)
                else:
                    e = width * len(gr)
                    nc.vector.tensor_tensor(pt_lo[:, sl, 0:e], b[:, 0:e], pt_hi[:, sl, 0:e].bitcast(F32),
                                            ALU.subtract).then_inc(s_ptlo, 1)
            v.wait_ge(s_o, i * N + s + 1)
            q, w_ = (P * t, P) if t < QT else (SEQ, NEW)
            ob = 512 * (6 + s % 2)
            if A:
                for m in (0, 1):
                    e = ob + P * m + P
                    ins = nc.vector.tensor_copy(c.o_col[64 * m:64 * m + 64, bass.ds(2 * i + g2, 1), q:q + w_],
                                                c.psum[64:128, e - w_:e].rearrange("p (a t) -> p a t", a=1))
            else:
                ins = nc.vector.tensor_copy(c.o_col[:, bass.ds(i, 1), q:q + w_],
                                            c.psum[:, ob + P - w_:ob + P].rearrange("p (a t) -> p a t", a=1))
            ins.then_inc(s_oe, 1)

        v.sem_inc(s_t, 1)
        v.sem_inc(s_ptlo, 1)
        v.sem_inc(s_oe, 1)
        v.sem_inc(s_nlo, 1)
        if not A:
            v.wait_ge(s_iota, 2)
            nc.vector.scalar_tensor_tensor(out=dist[:, :], in0=dist[:, :], scalar=-1.0, in1=dist[:, :],
                                           op0=ALU.mult, op1=ALU.max).then_inc(s_dist, 1)
            v.wait_ge(s_dist, 1)
            nc.vector.memset(dist[0:64, SEQ - CHUNK:SEQ], BIG).then_inc(s_dist, 1)
            v.wait_ge(s_dist, 2)
            nc.vector.tensor_scalar(dist[:, :], dist[:, :], 0.5, None, ALU.mult).then_inc(s_dist, 1)
            v.wait_ge(s_dist, 3)
        with v.Fori(0, passes) as i:
            if A:
                for t in range(PIECES):
                    v.wait_ge(s_phi, 9 * i + t + 1)
                    b = unit_banks[0][t]
                    src = c.psum[0:64, 512 * b:512 * b + TP]
                    nc.vector.tensor_tensor(k_lo[0:64, piece(t)], src, k_hi[0:64, piece(t)].bitcast(F32), ALU.subtract)
                    nc.vector.tensor_tensor(k_lo[64:128, piece(t)], src, k_hi[0:64, piece(t)].bitcast(F32),
                                            ALU.subtract).then_inc(s_plo, 1)
                for t in range(PIECES):
                    q_piece(i, 3 + t, t, 1, 0)
            else:
                for t in range(PIECES):
                    q_piece(i, t, t, 0, 0)
                for t in range(PIECES):
                    v.wait_ge(s_phi, 9 * i + 3 + t + 1)
                    nc.vector.tensor_tensor(k_lo[:, piece(t)], bank(c, unit_banks[1][t], TP),
                                            k_hi[:, piece(t)].bitcast(F32), ALU.subtract).then_inc(s_plo, 1)
            v.wait_ge(s_nhi, HI_ROWS * i + 1)
            nc.vector.tensor_tensor(v_lo[:, VCACHE, :], vc_nat[:, :], v_hi[:, VCACHE, :].bitcast(F32),
                                    ALU.subtract).then_inc(s_nlo, 1)
            for n in range(ROWGROUPS):
                b = bank(c, 4 + n % 2)
                r = n % 3
                rows = k_nat if A or n < 3 else v_nat
                if A or n >= 2:
                    v.wait_ge(s_nhi, HI_ROWS * i + (n + 2 if A else n))
                else:
                    v.wait_ge(s_nt, ROWGROUPS * i + n + 1)
                if n == 2:
                    if A:
                        for m in (0, 1):
                            nc.vector.tensor_tensor(k_lo[64 * m:64 * m + 64, TOK:KEYCOLS], b[0:64, P:2 * P],
                                                    k_hi[0:64, TOK:KEYCOLS].bitcast(F32), ALU.subtract)
                    else:
                        nc.vector.tensor_tensor(k_lo[:, TOK:KEYCOLS], b[:, P:2 * P],
                                                k_hi[:, TOK:KEYCOLS].bitcast(F32), ALU.subtract)
                if A or n >= 3:
                    if r < 2:
                        nc.vector.tensor_tensor(v_lo[:, 4 * r:4 * r + 4, :], b.rearrange("p (t d) -> p t d", t=4),
                                                v_hi[:, 4 * r:4 * r + 4, :].bitcast(F32), ALU.subtract)
                    else:
                        nc.vector.tensor_tensor(v_lo[0:NEW, VNEW, :], b[0:NEW, 0:P],
                                                v_hi[0:NEW, VNEW, :].bitcast(F32), ALU.subtract)
                if r < 2:
                    nc.vector.tensor_copy(rows[:, 4 * r:4 * r + 4, :], b.rearrange("p (t d) -> p t d", t=4)).then_inc(s_nlo, 1)
                else:
                    nc.vector.tensor_copy(rows[0:NEW, QT, :], b[0:NEW, 0:P]).then_inc(s_nlo, 1)
            for s in range(N + 2):
                if A and s == QT + 1:
                    for t in range(PIECES):
                        q_piece(i, 6 + t, t, 2, 1)
                if s < N:
                    read_logits(i, s)
                if s >= 2:
                    transposed(i, s - 2)
                if 1 <= s <= N:
                    normalise(i, s - 1)
            if A:
                nc.vector.tensor_scalar(c.bias[:, :], c.bias[:, :], 0.25, None, ALU.mult).then_inc(s_dist, 1)
                v.wait_ge(s_dist, i + 1)
            else:
                nc.vector.tensor_scalar(dist[:, :], dist[:, :], 0.5, None, ALU.mult).then_inc(s_dist, 1)
                v.wait_ge(s_dist, i + 4)

    return sync, pool, tensor, scalar, vector


def out_projection(c, kind):
    nc = c.nc
    name = "out" + kind
    o_hi = c.at("o_hi" + kind, [P, KC, TOK], F32R, 0)
    o_lo = c.at("o_lo" + kind, [P, KC, TOK], F32R, 33792)
    sq = c.at("o_sq" + kind, [P, KC, TP], F32, 67584)
    rr = c.at("o_rr" + kind, [P, KC, TP], F32, 0)
    S = lambda n: c.sem(n + kind)
    s_hi, s_lo, s_p, s_y = S("o_hi_done"), S("o_lo_done"), S("out_pieces"), S("out_added")
    if kind == "B":
        s_sq, s_ms, s_sd, s_rs = S("o_squares"), S("o_mean_sq"), S("o_root"), S("o_scaled")
    w = (c.dram["a_w_out"] if kind == "A" else c.dram["b_w_out"])[0].rearrange("(k p) n -> p k n", p=P)
    heads8 = c.psum[:, :].rearrange("p (h n) -> p h n", h=8)[:, :, 0:TP]

    def sync(sp):
        with sp.Fori(0, 4) as i:
            for u in (0, 1):
                load_unit(c, sp, name, i, u, [(whole, w[:, :, bass.ds(2 * P * i + P * u, P)])], KC)

    def pool(g):
        with g.Fori(0, 4) as i:
            for u in (0, 1):
                split_unit(c, g, name, i, u, KC)

    def tensor(pe):
        if kind == "B":
            for t in range(PIECES):
                pe.wait_ge(s_sq, t + 1)
                for h in range(BH):
                    mm = nc.tensor.matmul(bank(c, h, TP), c.mean_p[:, :], sq[:, h, :], start=True, stop=True)
                mm.then_inc(s_ms, 1)
        with pe.Fori(0, 4) as i:
            for u in (0, 1):
                s = unit_ready(c, pe, name, i, u)
                for t in range(PIECES):
                    pe.wait_ge(s_lo, t + 1)
                    pe.wait_ge(s_y, 6 * i + 3 * u + t + 1)
                    last = unit_product(c, bank(c, 3 * u + t, TP), s, KC, o_hi, o_lo, t)
                    piece_done(c, last, t, s_p, s)

    def scalar(act):
        if kind == "B":
            for t in range(PIECES):
                if t > 0:
                    act.wait_ge(s_rs, 3 * t)
                nc.scalar.activation(sq[:, :, :], c.o_col[:, :, piece(t)], ACT.Square).then_inc(s_sq, 1)
                act.wait_ge(s_ms, t + 1)
                nc.scalar.activation(rr[:, :, :], heads8, ACT.Sqrt, bias=c.eps[:, :]).then_inc(s_sd, 1)
            act.wait_ge(s_rs, 9)
        for t in range(PIECES):
            nc.scalar.activation(o_hi[:, :, piece(t)], c.o_col[:, :, piece(t)], ACT.Copy).then_inc(s_hi, 1)

    def vector(v):
        if kind == "B":
            for t in range(PIECES):
                o = c.o_col[:, :, piece(t)]
                v.wait_ge(s_sd, t + 1)
                nc.vector.reciprocal(rr[:, :, :], rr[:, :, :]).then_inc(s_rs, 1)
                v.wait_ge(s_rs, 3 * t + 1)
                nc.vector.tensor_tensor(o, o, rr[:, :, :], ALU.mult).then_inc(s_rs, 1)
                v.wait_ge(s_rs, 3 * t + 2)
                nc.vector.tensor_scalar(o, o, c.rms_gain[:, :], None, ALU.mult).then_inc(s_rs, 1)
        for t in range(PIECES):
            v.wait_ge(s_hi, t + 1)
            nc.vector.tensor_tensor(o_lo[:, :, piece(t)], c.o_col[:, :, piece(t)], o_hi[:, :, piece(t)].bitcast(F32),
                                    ALU.subtract).then_inc(s_lo, 1)
        v.wait_ge(s_lo, 3)
        v.sem_inc(s_y, 6)
        with v.Fori(0, 4) as i:
            for u in (0, 1):
                for t in range(PIECES):
                    n = 6 * i + 3 * u + t
                    y = c.o_col[:, bass.ds(2 * i + u, 1), piece(t)]
                    b = bank(c, 3 * u + t, TP).rearrange("p (a t) -> p a t", a=1)
                    await_piece(c, v, name, i, u, t, s_p, 2 * i + u)
                    nc.vector.scalar_tensor_tensor(out=y, in0=c.x_hi[:, bass.ds(2 * i + u, 1), piece(t)].bitcast(F32),
                                                   scalar=ALPHA, in1=b, op0=ALU.mult, op1=ALU.add).then_inc(s_y, 1)
                    v.wait_ge(s_y, n + 7)
                    nc.vector.scalar_tensor_tensor(out=y, in0=c.x_lo[:, bass.ds(2 * i + u, 1), piece(t)].bitcast(F32),
                                                   scalar=ALPHA, in1=y, op0=ALU.mult, op1=ALU.add)

    return sync, pool, tensor, scalar, vector


def layer_norm(c, layer, which):
    nc = c.nc
    tag = f"_{layer}{which}"
    sq = [c.at(f"ln_sq{j}{tag}", [P, KC, TP], F32, 11264 * j) for j in (0, 1)]
    sd = c.at("ln_sd" + tag, [P, TP], F32, 22528)
    names = ("ln_mean", "ln_centred", "ln_squares", "ln_var", "ln_root", "ln_steps", "ln_full", "ln_hi", "ln_lo")
    if not c.ln_sems:
        c.ln_sems = [c.sem(n) for n in names]
    s_mean, s_d, s_sq, s_var, s_sd, s_r, s_full, s_hi, s_lo = c.ln_sems
    done = PIECES * (2 * layer + which)
    last_one = (layer, which) == (DEPTH - 1, 1)
    par = lambda kind, k: c.params[:, 32 * kind + 16 * layer + 8 * which + k:32 * kind + 16 * layer + 8 * which + k + 1]

    def pool(g):
        if last_one:
            return
        for t in range(PIECES):
            g.wait_ge(s_full, KC * (done + t + 1))
            g.wait_ge(s_hi, KC * (done + t + 1))
            nc.gpsimd.tensor_tensor(c.x_lo[:, :, piece(t)], c.o_col[:, :, piece(t)],
                                    c.x_hi[:, :, piece(t)].bitcast(F32), ALU.subtract).then_inc(s_lo, 1)

    def tensor(pe):
        for t in range(PIECES):
            for k in range(KC):
                mm = nc.tensor.matmul(bank(c, t, TP), c.mean_d[:, :], c.o_col[:, k, piece(t)],
                                      start=(k == 0), stop=(k == KC - 1))
            mm.then_inc(s_mean, 1)
        for t in range(PIECES):
            pe.wait_ge(s_sq, done + t + 1)
            for k in range(KC):
                mm = nc.tensor.matmul(bank(c, 3 + t, TP), c.mean_d[:, :], sq[t % 2][:, k, :],
                                      start=(k == 0), stop=(k == KC - 1))
            mm.then_inc(s_var, 1)

    def scalar(act):
        for t in range(PIECES):
            act.wait_ge(s_d, done + t + 1)
            if t >= 2:
                act.wait_ge(s_var, done + t - 1)
            nc.scalar.activation(sq[t % 2][:, :, :], c.o_col[:, :, piece(t)], ACT.Square).then_inc(s_sq, 1)
        for t in range(PIECES):
            act.wait_ge(s_var, done + t + 1)
            if t >= 1:
                act.wait_ge(s_r, 2 * (done + t))
            nc.scalar.activation(sd[:, :], bank(c, 3 + t, TP), ACT.Sqrt, bias=c.eps[:, :]).then_inc(s_sd, 1)
            act.wait_ge(s_r, 2 * (done + t) + 2)
            if not last_one:
                for k in range(KC):
                    nc.scalar.activation(c.x_hi[:, k, piece(t)], c.o_col[:, k, piece(t)], ACT.Identity,
                                         bias=par(1, k), scale=par(0, k)).then_inc(s_hi, 1)

    def vector(v):
        for t in range(PIECES):
            v.wait_ge(s_mean, done + t + 1)
            o = c.o_col[:, :, piece(t)]
            mean = bank(c, t, TP).rearrange("p (a t) -> p a t", a=1).to_broadcast([P, KC, TP])
            nc.vector.tensor_tensor(o, o, mean, ALU.subtract).then_inc(s_d, 1)
        for t in range(PIECES):
            o = c.o_col[:, :, piece(t)]
            v.wait_ge(s_sd, done + t + 1)
            nc.vector.reciprocal(sd[:, :], sd[:, :]).then_inc(s_r, 1)
            v.wait_ge(s_r, 2 * (done + t) + 1)
            r = sd[:, :].rearrange("p (a t) -> p a t", a=1).to_broadcast([P, KC, TP])
            nc.vector.tensor_tensor(o, o, r, ALU.mult).then_inc(s_r, 1)
            v.wait_ge(s_r, 2 * (done + t) + 2)
            for k in range(KC):
                if not last_one:
                    v.wait_ge(s_hi, KC * (done + t) + k + 1)
                nc.vector.tensor_scalar(c.o_col[:, k, piece(t)], c.o_col[:, k, piece(t)], par(0, k), par(1, k),
                                        ALU.mult, ALU.add).then_inc(s_full, 1)

    def ready(eng):
        if not last_one:
            eng.wait_ge(s_lo, done + PIECES)
    return None, pool, tensor, scalar, vector, ready


def ffn(c, layer):
    nc = c.nc
    tag = str(layer)
    p_nat = c.at("p_nat" + tag, [P, QT + 1, PLE], F32, 0)
    p_hi, p_lo = c.at("p_hi" + tag, [P, 2, TOK], F32R, 9216), c.at("p_lo" + tag, [P, 2, TOK], F32R, 17664)
    h_hi, h_lo = c.at("h_hi" + tag, [P, 2, TOK], F32R, 26112), c.at("h_lo" + tag, [P, 2, TOK], F32R, 34560)
    gate = c.at("gate" + tag, [P, 2, TOK], F32, 43008)
    S = lambda n: c.sem(n + tag)
    s_pn, s_pt, s_ph, s_pl = S("p_loaded"), S("p_transposed"), S("p_hi_done"), S("p_lo_done")
    s_gp, s_sg, s_pp, s_t, s_acc = S("gate_pieces"), S("gate_done"), S("ple_pieces"), S("gated"), S("ple_added")
    s_g, s_si, s_u, s_h, s_hh, s_hl = S("ffn_gate"), S("silu_done"), S("ffn_up"), S("h_done"), S("h_hi_done"), S("h_lo_done")
    s_d, s_da = S("down_pieces"), S("down_added")
    wg = c.dram["ple_w_gate"][layer].rearrange("(k p) n -> p k n", p=P)
    wp = c.dram["ple_w_proj"][layer].rearrange("(k p) n -> p k n", p=P)
    w13 = c.dram["ffn_w13"][layer].rearrange("(k p) n -> p k n", p=P)
    w2 = c.dram["ffn_w2"][layer]
    ple, fn = "ple" + tag, "ffn" + tag
    PAIRS = DFF // P // 2
    no = c.phase_no

    def sync(sp):
        sp.wait_ge(c.phase_over, 3 * no)
        sp.dma_start(p_nat[:, 0:QT, :], c.dram["p_prompt"][layer, 0].rearrange("(t p) n -> p t n", p=P)).then_inc(s_pn, 16)
        sp.dma_start(p_nat[0:NEW, QT, :], c.dram["p_sample"][layer, 0]).then_inc(s_pn, 16)
        with sp.Fori(0, KC // 2) as i:
            for j in (0, 1):
                load_unit(c, sp, ple, i, 2 * j, [(whole, wg[:, :, bass.ds(2 * P * i + P * j, P)])], KC)
                load_unit(c, sp, ple, i, 2 * j + 1, [(whole, wp[:, :, bass.ds(2 * P * i + P * j, P)])], 2)
        with sp.Fori(0, PAIRS) as i:
            for j in (0, 1):
                load_unit(c, sp, fn, i, 2 * j, [(whole, w13[:, :, bass.ds(2 * P * i + P * j, P)])], KC)
                load_unit(c, sp, fn, i, 2 * j + 1, [(whole, w13[:, :, bass.ds(DFF + 2 * P * i + P * j, P)])], KC)
            for j in (0, 1):
                load_unit(c, sp, fn, i, 4 + j, [(lambda x: x.rearrange("p k n -> p (k n)"),
                                                 w2[bass.ds(2 * P * i + P * j, P), :])], KC)

    def pool(g):
        with g.Fori(0, KC // 2) as i:
            for j in (0, 1):
                split_unit(c, g, ple, i, 2 * j, KC)
                split_unit(c, g, ple, i, 2 * j + 1, 2)
        with g.Fori(0, PAIRS) as i:
            for u in range(6):
                split_unit(c, g, fn, i, u, KC)

    def tensor(pe):
        pe.wait_ge(s_pn, 32)
        for k in (0, 1):
            for b in (0, 1):
                for j in range(4):
                    mm = nc.tensor.transpose(bank(c, 2 * k + b)[:, P * j:P * j + P],
                                             p_nat[:, 4 * b + j, P * k:P * k + P], c.ident[:, :])
                mm.then_inc(s_pt, 1)
        for k in (0, 1):
            mm = nc.tensor.transpose(bank(c, 4)[:, NEW * k:NEW * k + NEW], p_nat[0:NEW, QT, P * k:P * k + P],
                                     c.ident[0:NEW, 0:NEW])
        mm.then_inc(s_pt, 1)
        pe.wait_ge(s_pl, 5)
        with pe.Fori(0, KC // 2) as i:
            for j in (0, 1):
                s = unit_ready(c, pe, ple, i, 2 * j)
                for t in range(PIECES):
                    pe.wait_ge(s_sg, 6 * i + 3 * j + t + 1)
                    last = unit_product(c, bank(c, t, TP), s, KC, c.x_hi, c.x_lo, t)
                    piece_done(c, last, t, s_gp, s)
                s = unit_ready(c, pe, ple, i, 2 * j + 1)
                for t in range(PIECES):
                    pe.wait_ge(s_t, 6 * i + 3 * j + t + 1)
                    last = unit_product(c, bank(c, 3 + t, TP), s, 2, p_hi, p_lo, t)
                    piece_done(c, last, t, s_pp, s)
        pe.wait_ge(s_t, 3 * KC + 3)
        with pe.Fori(0, PAIRS) as i:
            for j in (0, 1):
                s = unit_ready(c, pe, fn, i, 2 * j)
                for t in range(PIECES):
                    if j == 0:
                        pe.wait_ge(s_da, 24 * i + 19 + t)
                    pe.wait_ge(s_si, 6 * i + 3 * j + t + 1)
                    last = unit_product(c, bank(c, t, TP), s, KC, c.x_hi, c.x_lo, t)
                    piece_done(c, last, t, s_g, s)
                s = unit_ready(c, pe, fn, i, 2 * j + 1)
                for t in range(PIECES):
                    if j == 0:
                        pe.wait_ge(s_da, 24 * i + 22 + t)
                    pe.wait_ge(s_h, 6 * i + 3 * j + t + 1)
                    last = unit_product(c, bank(c, 3 + t, TP), s, KC, c.x_hi, c.x_lo, t)
                    piece_done(c, last, t, s_u, s)
            unit_ready(c, pe, fn, i, 4)
            unit_ready(c, pe, fn, i, 5)
            for t in range(PIECES):
                pe.wait_ge(s_hl, 6 * i + 3 + t + 1 + 3)
                for m in range(KC):
                    b = (6 + m) % 8
                    n = KC * t + m
                    if t > 0:
                        pe.wait_ge(s_da, 24 * i + 24 + n - 8 + 1)
                    elif b < 3:
                        pe.wait_ge(s_si, 6 * i + 3 + b + 1 + 3)
                    elif b < 6:
                        pe.wait_ge(s_h, 6 * i + 3 + (b - 3) + 1 + 3)
                    o, at_end = bank(c, b, TP), n == 3 * KC - 1
                    for j in (0, 1):
                        s = turn(fn, i, 4 + j)[0]
                        for k, (w, h) in enumerate(((c.w_hi, h_hi), (c.w_hi, h_lo), (c.w_lo, h_hi))):
                            mm = nc.tensor.matmul(o, w[s][:, m, :], h[:, j, piece(t)],
                                                  start=(j == 0 and k == 0), stop=(j == 1 and k == 2))
                        if at_end:
                            mm.then_inc(c.used[s], 1)
                    if not at_end:
                        mm.then_inc(s_d, 1)

    def scalar(act):
        for k in (0, 1):
            for b in (0, 1):
                act.wait_ge(s_pt, 2 * k + b + 1)
                nc.scalar.activation(p_hi[:, k, 512 * b:512 * b + 512], bank(c, 2 * k + b), ACT.Copy).then_inc(s_ph, 1)
        act.wait_ge(s_pt, 5)
        nc.scalar.activation(p_hi[:, :, SEQ:TOK], bank(c, 4, 2 * NEW).rearrange("p (k t) -> p k t", k=2), ACT.Copy).then_inc(s_ph, 1)
        act.sem_inc(s_sg, 3)
        act.sem_inc(s_si, 3)
        with act.Fori(0, KC // 2) as i:
            for j in (0, 1):
                for t in range(PIECES):
                    await_piece(c, act, ple, i, 2 * j, t, s_gp, 2 * i + j)
                    act.wait_ge(s_acc, 6 * i + 3 * j + t + 1)
                    nc.scalar.activation(gate[:, 0, piece(t)], bank(c, t, TP), ACT.Sigmoid).then_inc(s_sg, 1)
        act.wait_ge(s_acc, 3 * KC + 3)
        with act.Fori(0, PAIRS) as i:
            for j in (0, 1):
                for t in range(PIECES):
                    n = 6 * i + 3 * j + t
                    await_piece(c, act, fn, i, 2 * j, t, s_g, 2 * i + j)
                    act.wait_ge(s_hl, n + 1)
                    nc.scalar.activation(gate[:, 0, piece(t)], bank(c, t, TP), ACT.Silu).then_inc(s_si, 1)
                for t in range(PIECES):
                    act.wait_ge(s_h, 6 * i + 3 * j + t + 1 + 3)
                    nc.scalar.activation(h_hi[:, j, piece(t)], gate[:, 1, piece(t)], ACT.Copy).then_inc(s_hh, 1)

    def vector(v):
        for k in (0, 1):
            for b in (0, 1):
                v.wait_ge(s_ph, 2 * k + b + 1)
                nc.vector.tensor_tensor(p_lo[:, k, 512 * b:512 * b + 512], bank(c, 2 * k + b),
                                        p_hi[:, k, 512 * b:512 * b + 512].bitcast(F32), ALU.subtract).then_inc(s_pl, 1)
        v.wait_ge(s_ph, 5)
        nc.vector.tensor_tensor(p_lo[:, :, SEQ:TOK], bank(c, 4, 2 * NEW).rearrange("p (k t) -> p k t", k=2),
                                p_hi[:, :, SEQ:TOK].bitcast(F32), ALU.subtract).then_inc(s_pl, 1)
        v.sem_inc(s_t, 3)
        v.sem_inc(s_acc, 3)
        v.sem_inc(s_h, 3)
        v.sem_inc(s_hl, 3)
        v.sem_inc(s_da, 24)
        with v.Fori(0, KC // 2) as i:
            for j in (0, 1):
                for t in range(PIECES):
                    n = 6 * i + 3 * j + t
                    await_piece(c, v, ple, i, 2 * j + 1, t, s_pp, 2 * i + j)
                    v.wait_ge(s_sg, n + 1 + 3)
                    g = gate[:, 0, piece(t)]
                    nc.vector.tensor_tensor(g, bank(c, 3 + t, TP), g, ALU.mult).then_inc(s_t, 1)
                    v.wait_ge(s_t, n + 1 + 3)
                    o = c.o_col[:, bass.ds(2 * i + j, 1), piece(t)]
                    nc.vector.scalar_tensor_tensor(out=o, in0=o, scalar=ALPHA, in1=g.rearrange("p (a t) -> p a t", a=1),
                                                   op0=ALU.mult, op1=ALU.add).then_inc(s_acc, 1)
        with v.Fori(0, PAIRS) as i:
            for j in (0, 1):
                for t in range(PIECES):
                    n = 6 * i + 3 * j + t
                    await_piece(c, v, fn, i, 2 * j + 1, t, s_u, 2 * i + j)
                    v.wait_ge(s_si, n + 1 + 3)
                    v.wait_ge(s_hl, n + 1)
                    nc.vector.tensor_tensor(gate[:, 1, piece(t)], bank(c, 3 + t, TP), gate[:, 0, piece(t)],
                                            ALU.mult).then_inc(s_h, 1)
                for t in range(PIECES):
                    n = 6 * i + 3 * j + t
                    v.wait_ge(s_hh, n + 1)
                    nc.vector.tensor_tensor(h_lo[:, j, piece(t)], gate[:, 1, piece(t)],
                                            h_hi[:, j, piece(t)].bitcast(F32), ALU.subtract).then_inc(s_hl, 1)
            for t in range(PIECES):
                for m in range(KC):
                    if KC * t + m < 3 * KC - 1:
                        v.wait_ge(s_d, (3 * KC - 1) * i + KC * t + m + 1)
                    else:
                        s_, n_ = turn(fn, i, 5)
                        v.wait_ge(c.used[s_], n_ + 2)
                    o = c.o_col[:, m, piece(t)]
                    nc.vector.tensor_tensor(o, bank(c, (6 + m) % 8, TP), o, ALU.add).then_inc(s_da, 1)
        v.wait_ge(s_da, 24 * PAIRS + 24)

    return sync, pool, tensor, scalar, vector


def store_y(c):
    nc = c.nc
    rows = c.at("y_rows", [P, 4, D], F32, 32768)
    s_t, s_c, s_s = c.sem("y_transposed"), c.sem("y_copied"), [c.sem(f"y_stored{j}") for j in range(4)]

    def sync(sp):
        for t in range(QT + 1):
            n = P if t < QT else NEW
            sp.wait_ge(s_c, 2 * t + 2)
            dst = c.dram["y_prompt"][0, P * t:P * t + P, :] if t < QT else c.dram["y_sample"][0]
            sp.dma_start(dst, rows[0:n, t % 4, :]).then_inc(s_s[t % 4], 16)
        for j in range(4):
            sp.wait_ge(s_s[j], 16 * len(range(j, QT + 1, 4)))

    def tensor(pe):
        for t in range(QT + 1):
            n = P if t < QT else NEW
            for b in (0, 1):
                k = 2 * t + b
                if k >= 8:
                    pe.wait_ge(s_c, k - 7)
                for j in range(4):
                    mm = nc.tensor.transpose(bank(c, k % 8)[0:n, P * j:P * j + P],
                                             c.o_col[:, 4 * b + j, P * t:P * t + n], c.ident[:, :])
                mm.then_inc(s_t, 1)

    def scalar(act):
        for t in range(QT + 1):
            n = P if t < QT else NEW
            for b in (0, 1):
                k = 2 * t + b
                act.wait_ge(s_t, k + 1)
                if t >= 4:
                    act.wait_ge(s_s[t % 4], 16 * (t // 4))
                nc.scalar.activation(rows[0:n, t % 4, 512 * b:512 * b + 512], bank(c, k % 8)[0:n, :], ACT.Copy).then_inc(s_c, 1)

    return sync, None, tensor, scalar, None


INS = ['x_prompt', 'x_sample', 'cache_a_k', 'cache_a_v', 'cache_a_kidx', 'cache_b_k', 'cache_b_v',
       'p_prompt', 'p_sample', 'a_w_in', 'a_w_out', 'b_w_in', 'b_lambda', 'b_subln', 'b_w_out',
       'ffn_w13', 'ffn_w2', 'ple_w_proj', 'ple_w_gate', 'ln_gain', 'ln_bias']
OUTS = [('y_prompt', (1, SEQ, D)), ('y_sample', (1, NEW, D)),
        ('new_a_k_prompt', (1, 1, SEQ, KV, 64)), ('new_a_v_prompt', (1, 1, SEQ, KV, 64)),
        ('new_a_kidx_prompt', (1, 1, SEQ, IDXD)),
        ('new_b_k_prompt', (1, 1, SEQ, BH, P)), ('new_b_v_prompt', (1, 1, SEQ, BH, P)),
        ('new_a_k_sample', (1, 1, NEW, KV, 64)), ('new_a_v_sample', (1, 1, NEW, KV, 64)),
        ('new_a_kidx_sample', (1, 1, NEW, IDXD)),
        ('new_b_k_sample', (1, 1, NEW, BH, P)), ('new_b_v_sample', (1, 1, NEW, BH, P))]


def program(nc, drams):
    with ExitStack() as ctx:
        c = Core()
        c.nc = nc
        c.dram = drams
        c.sem = lambda n: ctx.enter_context(nc.semaphore(n))

        def sb(n, shape, dt=F32):
            return ctx.enter_context(nc.sbuf_tensor(n, shape, dt))

        c.x_rows = c.dram["x_prompt"].rearrange("b t d -> (b t) d")
        c.psum = ctx.enter_context(nc.psum_tensor("psum", [P, 8 * 512], F32))
        c.x_hi, c.x_lo = sb("x_hi", [P, KC, TOK], F32R), sb("x_lo", [P, KC, TOK], F32R)
        c.o_col = sb("o_col", [P, KC, TOK])
        c.w_raw = [sb(f"w_raw{s}", [P, KC, P]) for s in (0, 1)]
        c.w_hi = [sb(f"w_hi{s}", [P, KC, P], F32R) for s in (0, 1)]
        c.w_lo = [sb(f"w_lo{s}", [P, KC, P], F32R) for s in (0, 1)]
        c.zeros, c.ident = sb("zeros", [P, P]), sb("ident", [P, P])
        c.mean_d, c.mean_p = sb("mean_d", [P, P]), sb("mean_p", [P, P])
        c.q_scale, c.neg_sigma, c.neg_one = sb("q_scale", [P, 2]), sb("neg_sigma", [P, 2, 2]), sb("neg_one", [P, 2])
        c.eps, c.neg_lam, c.rms_gain = sb("eps", [P, 1]), sb("neg_lam", [P, 1]), sb("rms_gain", [P, 1])
        c.params, c.idx_w = sb("params", [P, 66]), sb("idx_w", [P, 9, 8])
        c.end = nc.sbuf_usable_end
        c.base = (nc.sbuf_base + 63) // 64 * 64
        arena = sb("arena", [P, (c.end - c.base) // 4 - 16])
        c.at = lambda n, shape, dt, off: nc.alloc_sbuf_tensor_at(n, shape, dt, offset=c.base + off)
        bias_cols = bias_at(QT) + PAST + NEW
        c.bias_bytes = 4 * bias_cols
        for s in (0, 1):
            c.w_raw.append(c.at(f"w_raw{s + 2}", [P, KC, P], F32, 51456 + 4096 * s))
            c.w_hi.append(c.at(f"w_hi{s + 2}", [P, KC, P], F32R, 59648 + 4096 * s))
            c.w_lo.append(c.at(f"w_lo{s + 2}", [P, KC, P], F32R, 67840 + 4096 * s))
        c.bias = c.at("bias", [P, bias_cols], F32, 0)
        c.dist = c.at("dist", [P, SEQ], F32, (c.end - c.base - 4096) // 64 * 64)
        c.loaded, c.split, c.used = ([c.sem(f"{n}{s}") for s in range(4)] for n in ("w_loaded", "w_split", "w_used"))
        c.phase_over = c.sem("phase_over")
        c.phase_no = 0
        c.ln_sems = None
        c.phases = []
        for make, *args in ((load_x,), (index_projection,), (selection,), (attention, "A"), (out_projection, "A"),
                            (layer_norm, 0, 0), (ffn, 0), (layer_norm, 0, 1), (attention, "B"), (out_projection, "B"),
                            (layer_norm, 1, 0), (ffn, 1), (layer_norm, 1, 1), (store_y,))[:LIMIT]:
            c.phase_no = len(c.phases)
            c.phases.append(make(c, *args))

        def compute(eng, which):
            for n, phase in enumerate(c.phases):
                if phase[which]:
                    phase[which](eng)
                eng.drain().then_inc(c.phase_over, 1)
                eng.wait_ge(c.phase_over, 3 * n + 3)
                for also in phase[5:]:
                    also(eng)

        block = ctx.enter_context(nc.Block())

        @block.sync
        def _(sp):
            for phase in c.phases:
                if phase[0]:
                    phase[0](sp)

        @block.gpsimd
        def _(pool):
            for phase in c.phases:
                if phase[1]:
                    phase[1](pool)

        @block.tensor
        def _(pe):
            compute(pe, 2)

        @block.scalar
        def _(act):
            compute(act, 3)

        @block.vector
        def _(dve):
            compute(dve, 4)


def kernel(**inputs):
    import numpy as _np
    import concourse.bacc as _bacc
    from concourse import mybir as _mybir
    from concourse.bass_utils import run_bass_kernel_spmd as _run

    nc = _bacc.Bacc("TRN2", target_bir_lowering=False, num_devices=1)
    arrays, drams = {}, {}
    for name in INS:
        a = _np.ascontiguousarray(inputs[name])
        arrays[f"in_{name}_dram"] = a
        drams[name] = nc.dram_tensor(f"in_{name}_dram", a.shape, _mybir.dt.from_np(a.dtype), kind="ExternalInput").ap()
    for name, shape in OUTS:
        drams[name] = nc.dram_tensor(f"out_{name}_dram", shape, F32, kind="ExternalOutput").ap()
    program(nc, drams)
    r = _run(nc, [arrays], core_ids=[0])
    return tuple(r.results[0][f"out_{name}_dram"] for name, _ in OUTS)
```

```python
import math
from contextlib import ExitStack

import concourse.bass as bass
from concourse import mybir

ALU = mybir.AluOpType
ACT = mybir.ActivationFunctionType
F32 = mybir.dt.float32
F32R = mybir.dt.float32r

P = 128
D = 1024
KC = D // P
SEQ, NEW, PAST = 1024, 32, 128
TOK = SEQ + NEW
PIECES = 3
TP = TOK // PIECES
QT = SEQ // P
SAMPLE = QT
CHUNK = 64
KV = 4
IDXH, IDXD = 8, 64
TOPK, TOPK_SAMPLE = 256, (PAST + NEW) // 4
BH = 8
DFF = 2816
PLE = 256
DEPTH = 2
LIMIT = 99
ALPHA = (2 * DEPTH) ** 0.25
EPS = 1e-5
BIG = 1.0e30
BARRED = -3.0e38
TAKEN = -3.3e38
TAKEN_BELOW = -3.2e38
LOWEST = -3.4e38
IDX_SCALE = IDXD ** -0.5 * IDXH ** -0.5
LAMBDA_INIT = 0.8 - 0.6 * math.exp(-0.3)
A_IN = 2120
QI0, KI0 = 1536, 2048

KEYCOLS = TOK + PAST
VBLK = QT + 2
VNEW, VCACHE = QT, QT + 1


def keys_of(tile):
    return P * (tile + 1) if tile < QT else PAST + NEW


def bias_at(tile):
    return P * tile * (tile + 1) // 2


def logit_parts(tile):
    if tile == SAMPLE:
        return [(0, P, TOK), (P, NEW, SEQ)]
    L = keys_of(tile)
    return [(a, max(256, min(512, L - a)), a) for a in range(0, L, 512)]


def first_query(tile):
    return P * tile if tile < QT else TOK - P


class Core:
    pass


def ring_plan():
    phases = [("index", 1, [0, 1, 0, 1, 0]), ("attnA", KV, [0, 1, 0]), ("outA", 4, [0, 1]),
              ("ple0", KC // 2, [0, 1, 2, 3]), ("ffn0", DFF // P // 2, [0, 1, 0, 1, 2, 3]),
              ("attnB", BH, [0, 1, 0]), ("outB", 4, [0, 1]),
              ("ple1", KC // 2, [0, 1, 2, 3]), ("ffn1", DFF // P // 2, [0, 1, 0, 1, 2, 3])]
    base, plan = [0] * 4, {}
    for name, passes, slots in phases:
        plan[name] = (tuple(base), slots)
        for s in range(4):
            base[s] += passes * slots.count(s)
    return plan


PLAN = ring_plan()


def turn(phase, i, u):
    base, slots = PLAN[phase]
    s = slots[u]
    return s, i * slots.count(s) + (base[s] + slots[:u].count(s))


def load_unit(c, sp, phase, i, u, parts, kc):
    s, n = turn(phase, i, u)
    sp.wait_ge(c.split[s], 2 * n + 2)
    for dst, src in parts:
        sp.dma_start(dst(c.w_raw[s][:, 0:kc]), src).then_inc(c.loaded[s], 32 // len(parts))


def whole(t):
    return t


def split_unit(c, pool, phase, i, u, kc):
    s, n = turn(phase, i, u)
    pool.wait_ge(c.loaded[s], 32 * n + 32)
    pool.wait_ge(c.used[s], n + 1)
    nc = c.nc
    zero = c.zeros[:, :].rearrange("p (a b) -> p a b", a=1).to_broadcast([P, kc, P])
    nc.gpsimd.tensor_tensor(c.w_hi[s][:, 0:kc], c.w_raw[s][:, 0:kc], zero, ALU.add).then_inc(c.split[s], 1)
    pool.wait_ge(c.split[s], 2 * n + 3)
    nc.gpsimd.tensor_tensor(c.w_lo[s][:, 0:kc], c.w_raw[s][:, 0:kc], c.w_hi[s][:, 0:kc].bitcast(F32),
                            ALU.subtract).then_inc(c.split[s], 1)


def unit_ready(c, pe, phase, i, u):
    s, n = turn(phase, i, u)
    pe.wait_ge(c.split[s], 2 * n + 4)
    return s


def piece_done(c, mm, t, sem, s):
    mm.then_inc(sem, 1) if t < PIECES - 1 else mm.then_inc(c.used[s], 1)


def await_piece(c, eng, phase, i, u, t, sem, before):
    if t < PIECES - 1:
        eng.wait_ge(sem, 2 * before + t + 1)
    else:
        s, n = turn(phase, i, u)
        eng.wait_ge(c.used[s], n + 2)


def product(c, out, terms):
    last, n = None, 0
    for (wh, wl), (xh, xl) in terms:
        for w, x in ((wh, xh), (wh, xl), (wl, xh)):
            last = c.nc.tensor.matmul(out, w, x, start=(n == 0), stop=(n == 3 * len(terms) - 1))
            n += 1
    return last


def unit_product(c, out, s, kc, xh, xl, t, cols=P):
    return product(c, out, [((c.w_hi[s][:, k, 0:cols], c.w_lo[s][:, k, 0:cols]),
                             (xh[:, k, piece(t)], xl[:, k, piece(t)])) for k in range(kc)])


def piece(t):
    return slice(TP * t, TP * t + TP)


def bank(c, b, n=512):
    return c.psum[:, 512 * b:512 * b + n]


def load_x(c):
    nc = c.nc
    nat = c.at("x_nat", [P, 2, D], F32, 0)
    par = c.at("ln_rows", [66, P], F32, 8192)
    lam = c.at("lam_rows", [P, 4 * 64], F32, 8704)
    lamp = c.at("lam_prod", [P, 64], F32, 9728)
    lsum = c.at("lam_sum", [P, 4], F32, 9984)
    s_nat = [c.sem("x_loaded0"), c.sem("x_loaded1")]
    s_tail, s_par = c.sem("x_sample_loaded"), c.sem("params_loaded")
    s_t, s_hi, s_lo = c.sem("x_transposed"), c.sem("x_hi_done"), c.sem("x_lo_done")
    s_c, s_l = c.sem("const_steps"), c.sem("lambda_steps")
    x = c.dram["x_prompt"].rearrange("b (t p) d -> (b t) p d", p=P)

    def sync(sp):
        sp.dma_start(nat[:, 0], x[0]).then_inc(s_nat[0], 16)
        sp.dma_start(nat[:, 1], x[1]).then_inc(s_nat[1], 16)
        sp.dma_start(par[0:32, :], c.dram["ln_gain"].rearrange("l w (k p) -> (l w k) p", p=P)).then_inc(s_par, 16)
        sp.dma_start(par[32:64, :], c.dram["ln_bias"].rearrange("l w (k p) -> (l w k) p", p=P)).then_inc(s_par, 16)
        sp.dma_start(par[64:65, :], c.dram["b_subln"]).then_inc(s_par, 16)
        sp.dma_start(par[65:66, :], c.dram["b_subln"]).then_inc(s_par, 16)
        sp.dma_start(lam[:, :], c.dram["b_lambda"].rearrange("l a d -> l (a d)").to_broadcast([P, 256])).then_inc(s_par, 16)
        with sp.Fori(0, 3) as i:
            for j in (0, 1):
                sp.wait_ge(s_t, 4 * i + 2 * j + 6)
                sp.dma_start(nat[:, j], c.x_rows[bass.ds(2 * P * i + P * (2 + j), P), :]).then_inc(s_nat[j], 16)
        sp.wait_ge(s_t, 4 + 4 * 3 + 2)
        sp.dma_start(nat[0:NEW, 0], c.dram["x_sample"].rearrange("b t d -> (b t) d")).then_inc(s_tail, 16)

    def pool(g):
        nc.gpsimd.memset(c.zeros[:, :], 0.0).then_inc(s_c, 1)
        nc.gpsimd.memset(c.ident[:, :], 0.0).then_inc(s_c, 1)
        nc.gpsimd.memset(c.mean_d[:, :], 1.0 / D).then_inc(s_c, 1)
        nc.gpsimd.memset(c.eps[:, :], EPS).then_inc(s_c, 1)
        nc.gpsimd.memset(c.neg_one[:, :], -1.0).then_inc(s_c, 1)
        g.wait_ge(s_c, 5)
        nc.gpsimd.affine_select(out=c.ident[:, :], in_=c.ident[:, :], compare_op=ALU.not_equal, fill=1.0,
                                base=0, pattern=[[-1, P]], channel_multiplier=1).then_inc(s_c, 1)
        nc.gpsimd.iota(c.dist[:, :], pattern=[[-1, SEQ]], base=SEQ - P, channel_multiplier=1,
                       allow_small_or_imprecise_dtypes=True).then_inc(s_c, 1)
        for s in range(4):
            g.sem_inc(c.split[s], 2)

    def tensor(pe):
        for s in range(4):
            pe.sem_inc(c.used[s], 1)
        pe.sem_inc(s_t, 4)
        pe.wait_ge(s_c, 6)
        with pe.Fori(0, 4) as i:
            for j in (0, 1):
                pe.wait_ge(s_nat[j], 16 * i + 16)
                for b in (0, 1):
                    pe.wait_ge(s_lo, 4 * i + 2 * j + b + 1)
                    for k in range(4):
                        mm = nc.tensor.transpose(bank(c, 2 * j + b)[:, P * k:P * k + P],
                                                 nat[:, j, P * (4 * b + k):P * (4 * b + k) + P], c.ident[:, :])
                    mm.then_inc(s_t, 1)
        pe.wait_ge(s_tail, 16)
        for k in range(KC):
            mm = nc.tensor.transpose(bank(c, 4)[:, NEW * k:NEW * k + NEW], nat[0:NEW, 0, P * k:P * k + P],
                                     c.ident[0:NEW, 0:NEW])
        mm.then_inc(s_t, 1)
        pe.wait_ge(s_par, 80)
        nc.tensor.transpose(bank(c, 5)[:, 0:66], par[:, :], c.ident[0:66, 0:66]).then_inc(s_t, 1)

    def places(i, j):
        for b in (0, 1):
            yield 2 * j + b, (slice(4 * b, 4 * b + 4), bass.ds(2 * P * i + P * j, P)), b

    def scalar(act):
        with act.Fori(0, 4) as i:
            for j in (0, 1):
                for bk, (ks, ts), b in places(i, j):
                    act.wait_ge(s_t, 4 * i + 2 * j + b + 5)
                    nc.scalar.activation(c.x_hi[:, ks, ts], bank(c, bk).rearrange("p (k t) -> p k t", k=4),
                                         ACT.Copy).then_inc(s_hi, 1)
        act.wait_ge(s_t, 21)
        nc.scalar.activation(c.x_hi[:, :, SEQ:TOK], bank(c, 4, KC * NEW).rearrange("p (k t) -> p k t", k=KC),
                             ACT.Copy).then_inc(s_hi, 1)
        act.wait_ge(s_l, 2)
        nc.scalar.activation(lsum[:, 2:4], lsum[:, 0:2], ACT.Exp).then_inc(s_l, 1)

    def vector(v):
        v.sem_inc(s_lo, 4)
        for g2 in (0, 1):
            for m in (0, 1):
                sigma = 2.0 ** (-(2 * g2 + m + 1) / 2)
                nc.vector.memset(c.q_scale[64 * m:64 * m + 64, g2:g2 + 1], 0.125 / sigma)
                nc.vector.memset(c.neg_sigma[:, g2, m:m + 1], -sigma)
        with v.Fori(0, 4) as i:
            for j in (0, 1):
                for bk, (ks, ts), b in places(i, j):
                    v.wait_ge(s_hi, 4 * i + 2 * j + b + 1)
                    nc.vector.tensor_tensor(c.x_lo[:, ks, ts], bank(c, bk).rearrange("p (k t) -> p k t", k=4),
                                            c.x_hi[:, ks, ts].bitcast(F32), ALU.subtract).then_inc(s_lo, 1)
        v.wait_ge(s_hi, 17)
        nc.vector.tensor_tensor(c.x_lo[:, :, SEQ:TOK], bank(c, 4, KC * NEW).rearrange("p (k t) -> p k t", k=KC),
                                c.x_hi[:, :, SEQ:TOK].bitcast(F32), ALU.subtract).then_inc(s_lo, 1)
        v.wait_ge(s_t, 22)
        nc.vector.tensor_copy(c.params[:, :], bank(c, 5, 66)).then_inc(s_lo, 1)
        v.wait_ge(s_lo, 22)
        nc.vector.tensor_scalar(c.rms_gain[:, :], c.params[:, 64:65], 1.0 - LAMBDA_INIT, None,
                                ALU.mult).then_inc(s_lo, 1)
        v.wait_ge(s_c, 7)
        nc.vector.scalar_tensor_tensor(out=c.dist[:, :], in0=c.dist[:, :], scalar=-1.0, in1=c.dist[:, :],
                                       op0=ALU.mult, op1=ALU.max).then_inc(s_lo, 1)
        v.wait_ge(s_par, 80)
        for m in (0, 1):
            nc.vector.tensor_tensor_reduce(lamp[:, :], lam[:, P * m:P * m + 64], lam[:, P * m + 64:P * m + P],
                                           1.0, 0.0, ALU.mult, ALU.add, lsum[:, m:m + 1]).then_inc(s_l, 1)
            v.wait_ge(s_l, m + 1)
        v.wait_ge(s_l, 3)
        nc.vector.tensor_tensor(c.neg_lam[:, :], lsum[:, 3:4], lsum[:, 2:3], ALU.subtract).then_inc(s_l, 1)
        v.wait_ge(s_l, 4)
        nc.vector.tensor_scalar(c.neg_lam[:, :], c.neg_lam[:, :], -LAMBDA_INIT, None, ALU.add).then_inc(s_l, 1)

    return sync, pool, tensor, scalar, vector


def index_projection(c):
    nc = c.nc
    base = c.bias_bytes
    qi_hi = c.at("qi_hi", [P, 4, TOK], F32R, base)
    qi_lo = c.at("qi_lo", [P, 4, TOK], F32R, base + 16896)
    ki_hi = c.at("ki_hi", [P, KEYCOLS], F32R, base + 33792)
    ki_lo = c.at("ki_lo", [P, KEYCOLS], F32R, base + 38528)
    kw = c.at("kiw", [72, TOK], F32, base + 43264)
    kw_nat = c.at("kiw_nat", [P, 9, 72], F32, base + 47488)
    cache = c.at("kidx_cache", [P, IDXD], F32, base + 50080)
    c.qi, c.ki, c.kw_nat = (qi_hi, qi_lo), (ki_hi, ki_lo), kw_nat
    c.idx_free = base + 50336
    s_p, s_hi, s_lo = c.sem("idx_pieces"), c.sem("idx_hi_done"), c.sem("idx_lo_done")
    s_kw, s_nt, s_nat = c.sem("kiw_copied"), c.sem("kiw_transposed"), c.sem("kiw_nat_done")
    s_ca, s_out = c.sem("kidx_cache_loaded"), c.sem("kidx_stored")
    w = c.dram["a_w_in"][0].rearrange("(k p) n -> p k n", p=P)

    def sync(sp):
        for u in range(4):
            load_unit(c, sp, "index", 0, u, [(whole, w[:, :, QI0 + P * u:QI0 + P * u + P])], KC)
        load_unit(c, sp, "index", 0, 4, [(lambda t: t[:, :, 0:72], w[:, :, KI0:KI0 + 72])], KC)
        sp.wait_ge(c.phase_over, 3)
        sp.dma_start(cache[:, :], c.dram["cache_a_kidx"][0, 0]).then_inc(s_ca, 16)
        sp.wait_ge(s_nat, 2)
        sp.dma_start(c.dram["new_a_kidx_prompt"][0, 0].rearrange("(t p) d -> p t d", p=P),
                     kw_nat[:, 0:QT, 0:IDXD]).then_inc(s_out, 16)
        sp.dma_start(c.dram["new_a_kidx_sample"][0, 0], kw_nat[P - NEW:P, QT, 0:IDXD]).then_inc(s_out, 16)

    def pool(g):
        for u in range(5):
            split_unit(c, g, "index", 0, u, KC)

    def tensor(pe):
        for u in range(5):
            s = unit_ready(c, pe, "index", 0, u)
            for t in range(PIECES):
                b = 3 * (u % 2) + t
                if u >= 2:
                    pe.wait_ge(s_lo, 3 * (u - 2) + t + 1)
                last = unit_product(c, bank(c, b, TP) if u < 4 else c.psum[0:72, 512 * b:512 * b + TP], s, KC,
                                    c.x_hi, c.x_lo, t, P if u < 4 else 72)
                piece_done(c, last, t, s_p, s)
        pe.wait_ge(s_ca, 16)
        pe.wait_ge(s_lo, 12)
        nc.tensor.transpose(c.psum[0:64, 512 * 3:512 * 3 + P], cache[:, :], c.ident[:, :]).then_inc(s_nt, 1)
        pe.wait_ge(s_kw, 3)
        for t in range(9):
            b, at = (6, t) if t < 7 else (7, t - 7)
            q = first_query(t)
            mm = nc.tensor.transpose(bank(c, b)[:, 72 * at:72 * at + 72], kw[:, q:q + P], c.ident[0:72, 0:72])
            if t in (6, 8):
                mm.then_inc(s_nt, 1)

    def scalar(act):
        for u in range(4):
            for t in range(PIECES):
                await_piece(c, act, "index", 0, u, t, s_p, u)
                nc.scalar.activation(qi_hi[:, u, piece(t)], bank(c, 3 * (u % 2) + t, TP), ACT.Copy).then_inc(s_hi, 1)
        for t in range(PIECES):
            await_piece(c, act, "index", 0, 4, t, s_p, 4)
            src = c.psum[0:64, 512 * t:512 * t + TP]
            nc.scalar.activation(kw[:, piece(t)], c.psum[0:72, 512 * t:512 * t + TP], ACT.Copy).then_inc(s_kw, 1)
            nc.scalar.activation(ki_hi[0:64, piece(t)], src, ACT.Copy).then_inc(s_hi, 1)
            nc.scalar.activation(ki_hi[64:128, piece(t)], src, ACT.Copy).then_inc(s_hi, 1)
        act.wait_ge(s_nt, 1)
        for m in (0, 1):
            nc.scalar.activation(ki_hi[64 * m:64 * m + 64, TOK:KEYCOLS], c.psum[0:64, 512 * 3:512 * 3 + P],
                                 ACT.Copy).then_inc(s_hi, 1)

    def vector(v):
        for u in range(4):
            for t in range(PIECES):
                v.wait_ge(s_hi, 3 * u + t + 1)
                nc.vector.tensor_tensor(qi_lo[:, u, piece(t)], bank(c, 3 * (u % 2) + t, TP),
                                        qi_hi[:, u, piece(t)].bitcast(F32), ALU.subtract).then_inc(s_lo, 1)
        for t in range(PIECES):
            v.wait_ge(s_hi, 12 + 2 * t + 2)
            for m in (0, 1):
                nc.vector.tensor_tensor(ki_lo[64 * m:64 * m + 64, piece(t)], c.psum[0:64, 512 * t:512 * t + TP],
                                        ki_hi[0:64, piece(t)].bitcast(F32), ALU.subtract).then_inc(s_lo, 1)
        v.wait_ge(s_hi, 20)
        for m in (0, 1):
            nc.vector.tensor_tensor(ki_lo[64 * m:64 * m + 64, TOK:KEYCOLS], c.psum[0:64, 512 * 3:512 * 3 + P],
                                    ki_hi[0:64, TOK:KEYCOLS].bitcast(F32), ALU.subtract).then_inc(s_lo, 1)
        v.wait_ge(s_nt, 3)
        nc.vector.tensor_copy(kw_nat[:, 0:7, :], bank(c, 6, 504).rearrange("p (t n) -> p t n", n=72)).then_inc(s_nat, 1)
        nc.vector.tensor_copy(kw_nat[:, 7:9, :], bank(c, 7, 144).rearrange("p (t n) -> p t n", n=72)).then_inc(s_nat, 1)
        v.wait_ge(s_nat, 2)
        nc.vector.tensor_scalar(c.idx_w[:, :, :], kw_nat[:, :, 64:72], IDX_SCALE, None, ALU.mult).then_inc(s_nat, 1)

    c.kidx_stored = lambda eng: eng.wait_ge(s_out, 32)
    return sync, pool, tensor, scalar, vector


def selection(c):
    nc = c.nc
    relu = [c.at(f"relu{j}", [P, SEQ], F32, c.idx_free + 4096 * j) for j in (0, 1)]
    top8 = c.at("top8", [P, 8], F32, c.idx_free + 8192)
    s_dot, s_relu, s_acc, s_top = c.sem("dots"), c.sem("relu_done"), c.sem("scores_added"), c.sem("top_steps")
    ranked = list(range(2, QT)) + [SAMPLE]
    work = [(t, h) for t in ranked for h in range(IDXH)]

    def dist_of(t, n):
        at = P * (QT - 1 - t) if t < QT else (SEQ - P) - 32
        return c.dist[:, at:at + n]

    def tensor(pe):
        for n, (t, h) in enumerate(work):
            L, q, ch, m = keys_of(t), first_query(t), h // 2, h % 2
            if n >= 4:
                pe.wait_ge(s_relu, n - 3)
            rows = slice(64 * m, 64 * m + 64)
            parts = logit_parts(t)
            for at, w, key in parts:
                o = c.psum[:, 1024 * (n % 4) + at:1024 * (n % 4) + at + w]
                last = product(c, o, [((c.qi[0][rows, ch, q:q + P], c.qi[1][rows, ch, q:q + P]),
                                       (c.ki[0][rows, key:key + w], c.ki[1][rows, key:key + w]))])
            last.then_inc(s_dot, 1)

    def scalar(act):
        for n, (t, h) in enumerate(work):
            L = keys_of(t)
            act.wait_ge(s_dot, n + 1)
            if n >= 2:
                act.wait_ge(s_acc, n - 1)
            nc.scalar.activation(relu[n % 2][:, 0:L], c.psum[:, 1024 * (n % 4):1024 * (n % 4) + L],
                                 ACT.Relu).then_inc(s_relu, 1)

    def vector(v):
        for t in (0, 1):
            L = keys_of(t)
            o = c.bias[:, bias_at(t):bias_at(t) + L]
            nc.vector.tensor_copy(o, dist_of(t, L)).then_inc(s_top, 1)
        v.wait_ge(s_top, 2)
        for t in (0, 1):
            e = bias_at(t) + keys_of(t)
            nc.vector.memset(c.bias[0:64, e - CHUNK:e], BIG).then_inc(s_top, 1)
        step = 4
        for n, (t, h) in enumerate(work):
            L = keys_of(t)
            score = c.bias[:, bias_at(t):bias_at(t) + L]
            v.wait_ge(s_relu, n + 1)
            weight = c.idx_w[:, t, h:h + 1]
            if h == 0:
                nc.vector.tensor_scalar(score, relu[n % 2][:, 0:L], weight, None, ALU.mult).then_inc(s_acc, 1)
            else:
                v.wait_ge(s_acc, n)
                nc.vector.scalar_tensor_tensor(out=score, in0=relu[n % 2][:, 0:L], scalar=weight, in1=score,
                                               op0=ALU.mult, op1=ALU.add).then_inc(s_acc, 1)
        for t in ranked:
            L = keys_of(t)
            score = c.bias[:, bias_at(t):bias_at(t) + L]
            v.wait_ge(s_acc, len(work))
            if t < QT:
                nc.vector.memset(c.bias[0:64, bias_at(t) + L - CHUNK:bias_at(t) + L], BARRED).then_inc(s_top, 1)
                step += 1
            v.wait_ge(s_top, step)
            rounds = (TOPK if t < QT else TOPK_SAMPLE) // 8
            for r in range(rounds):
                v.wait_ge(s_top, step + 2 * r)
                nc.vector.max(top8[:, :], score).then_inc(s_top, 1)
                v.wait_ge(s_top, step + 2 * r + 1)
                nc.vector.match_replace(score, top8[:, :], score, TAKEN).then_inc(s_top, 1)
            step += 2 * rounds
            v.wait_ge(s_top, step)
            nc.vector.tensor_scalar(score, score, TAKEN_BELOW, BIG, ALU.is_ge, ALU.mult).then_inc(s_top, 1)
            step += 1
            v.wait_ge(s_top, step)
            nc.vector.tensor_tensor(score, score, dist_of(t, L), ALU.add).then_inc(s_top, 1)
            step += 1
        v.wait_ge(s_top, step)

    return None, None, tensor, scalar, vector, c.kidx_stored


def attention(c, kind):
    nc = c.nc
    A = kind == "A"
    name = "attn" + kind
    passes = KV if A else BH
    steps = [(g2, t) for g2 in ((0, 1) if A else (0,)) for t in range(QT + 1)]
    N = len(steps)
    no = c.phase_no
    at = c.bias_bytes if A else 0
    def place(nm, shape, dt, size=None):
        nonlocal at
        t = c.at(nm + kind, shape, dt, at)
        n = 4
        for x in shape[1:]:
            n *= x
        at += -(-n // 32) * 32
        return t
    q_hi, q_lo = place("q_hi", [P, TOK], F32R), place("q_lo", [P, TOK], F32R)
    k_hi, k_lo = place("k_hi", [P, KEYCOLS], F32R), place("k_lo", [P, KEYCOLS], F32R)
    v_hi, v_lo = place("v_hi", [P, VBLK, P], F32R), place("v_lo", [P, VBLK, P], F32R)
    slots = 3
    wide = 2 * P if A else P
    pt = place("pt", [P, slots, 512 // wide, 2, wide], F32R)
    kc_nat = place("k_cache", [P, P], F32)
    vc_nat = kc_nat if A else place("v_cache", [P, P], F32)
    v_nat = None if A else place("v_nat", [P, 9, P], F32)
    if not A:
        dist = place("dist", [P, SEQ + PAST + NEW], F32)
    stat = place("stat", [P, 3, 10], F32)
    p_at = at
    prob = place("prob", [P, 3, 2, SEQ], F32)
    v_col = c.at("v_col" + kind, [P, TOK], F32, p_at)
    k_col = v_col if A else c.at("k_colB", [P, TOK], F32, p_at + 8192)
    k_nat = c.at("k_nat" + kind, [P, 9, P], F32, p_at + 16384)
    assert c.base + at <= c.end, (c.base + at, c.end)

    S = lambda n: c.sem(n + kind)
    s_piece, s_phi, s_plo = S("pieces"), S("pieces_hi"), S("pieces_lo")
    s_nt, s_nhi, s_nlo = S("rows_transposed"), S("rows_hi"), S("rows_done")
    s_cache, s_out = S("cache_loaded"), S("rows_stored")
    s_s, s_t, s_nb, s_exp, s_norm = S("logits"), S("logits_read"), S("row_max"), S("exp_done"), S("probs_ready")
    s_small, s_cleared = S("small_steps"), S("max_cleared")
    s_pt, s_pthi, s_ptlo = S("probs_transposed"), S("probsT_hi"), S("probsT_lo")
    s_o, s_oe = S("outputs"), S("outputs_read")
    s_dist, s_iota = S("dist_scaled"), S("dist_counted")
    s_first = None if A else S("outputs_copied")

    per = 2 if A else 4
    def blocks(t):
        return list(range(t + 1)) if t < QT else [VCACHE, VNEW]
    def groups(t):
        b = blocks(t)
        return [b[j:j + per] for j in range(0, len(b), per)]
    first_group, g = [], 0
    for _, t in steps:
        first_group.append(g)
        g += len(groups(t))
    GROUPS = g
    wd = 64 if A else P

    def columns(a, at):
        return a[0, 0].rearrange("s h d -> s (h d)")[:, bass.ds(at, wd)]

    LOS = 9 if A else 6
    turn_banks = (4, 5, 7)
    unit_banks = [[0, 1, 2], [3, 6, 7], [0, 1, 2 if A else 6]]
    ROWGROUPS = 3 if A else 6
    w = (c.dram["a_w_in"] if A else c.dram["b_w_in"])[0].rearrange("(k p) n -> p k n", p=P)

    def sync(sp):
        def weights(start, width, at):
            return w[:, :, start:][:, :, bass.ds(at, width)]

        with sp.Fori(0, passes) as i:
            head, pair = sp.snap(i * wd), sp.snap(i * 2 * P)
            if A:
                load_unit(c, sp, name, i, 0, [(lambda x: x[:, :, 0:64], weights(1024, 64, head)),
                                              (lambda x: x[:, :, 64:128], weights(1280, 64, head))], KC)
                load_unit(c, sp, name, i, 1, [(whole, weights(0, P, pair))], KC)
            else:
                v_at, k_at = sp.snap(i * P + 2 * D), sp.snap(i * P + D)
                load_unit(c, sp, name, i, 0, [(whole, weights(0, P, v_at))], KC)
                load_unit(c, sp, name, i, 1, [(whole, weights(0, P, k_at))], KC)
            load_unit(c, sp, name, i, 2, [(whole, weights(P, P, pair) if A else weights(0, P, (i + BH) * P - D))], KC)
        sp.wait_ge(s_out, 64 * passes)

    def pool(g):
        if not A:
            g.wait_ge(c.phase_over, 3 * no)
            nc.gpsimd.iota(dist[:, 0:SEQ], pattern=[[-1, SEQ]], base=SEQ - P, channel_multiplier=1,
                           allow_small_or_imprecise_dtypes=True).then_inc(s_iota, 1)
            nc.gpsimd.iota(dist[:, SEQ:], pattern=[[-1, PAST + NEW]], base=NEW, channel_multiplier=1,
                           allow_small_or_imprecise_dtypes=True).then_inc(s_iota, 1)
        with g.Fori(0, passes) as i:
            for u in range(3):
                split_unit(c, g, name, i, u, KC)

    def tensor(pe):
        def unit(i, u, pieces=range(PIECES)):
            s = unit_ready(c, pe, name, i, u)
            for t in pieces:
                o = bank(c, unit_banks[u][t], TP)
                last = unit_product(c, o, s, KC, c.x_hi, c.x_lo, t)
                piece_done(c, last, t, s_piece, s)

        def row_group(i, n, src, tiles, extra=None):
            b = bank(c, 4 + n % 2)
            if n >= 2:
                pe.wait_ge(s_nlo, (ROWGROUPS + 1) * i + n + 1)
            for j, t in enumerate(tiles):
                cols = P if t < QT else NEW
                mm = nc.tensor.transpose(b[0:cols, P * j:P * j + P], src[:, P * t:P * t + cols], c.ident[:, :])
            if extra is not None:
                mm = nc.tensor.transpose(b[:, P:2 * P], extra[:, :], c.ident[:, :])
            mm.then_inc(s_nt, 1)

        def logits(i, s, m):
            t = steps[s][1]
            L, q = keys_of(t), first_query(t)
            parts = logit_parts(t)
            if s > 0:
                pe.wait_ge(s_t, i * 2 * N + 2 * (s - 1) + m + 1 + 1)
            rows = slice(64 * m, 64 * m + 64)
            for a, n, key in parts:
                o = c.psum[:, 1024 * m + a:1024 * m + a + n]
                last = product(c, o, [((q_hi[rows, q:q + P], q_lo[rows, q:q + P]),
                                       (k_hi[rows, key:key + n], k_lo[rows, key:key + n]))])
            last.then_inc(s_s, 1)

        def turn_over(i, s, j):
            t = steps[s][1]
            n = first_group[s] + j
            if n >= 3:
                pe.wait_ge(s_ptlo, i * GROUPS + n - 3 + 1 + 1)
            b = bank(c, turn_banks[n % 3])
            for x, blk in enumerate(groups(t)[j]):
                key = P * (per * j + x)
                w_ = NEW if blk == VNEW else P
                for m in range(2 if A else 1):
                    col = P * ((2 * x + m) if A else x)
                    mm = nc.tensor.transpose(b[0:w_, col:col + P], prob[:, s % 3, m, key:key + w_], c.ident[:, :])
            mm.then_inc(s_pt, 1)

        def multiply(i, s, j):
            gs = groups(steps[s][1])
            n = first_group[s] + j
            pe.wait_ge(s_ptlo, i * GROUPS + n + 1 + 1)
            sl, o = n % slots, 512 * 6
            for x, blk in enumerate(gs[j]):
                r = slice(0, NEW if blk == VNEW else P)
                first, lastb = (j == 0 and x == 0), (j == len(gs) - 1 and x == len(gs[j]) - 1)
                if A:
                    terms = [(v_hi, pt[r, sl, x, 0]), (v_hi, pt[r, sl, x, 1]), (v_lo, pt[r, sl, x, 0])]
                else:
                    terms = [(vv, pt[r, sl, x].rearrange("p a q -> p (a q)")) for vv in (v_hi, v_lo)]
                for k, (vv, pp) in enumerate(terms):
                    mm = nc.tensor.matmul(c.psum[:, o:o + 2 * P], vv[r, blk, :], pp,
                                          start=(first and k == 0), stop=(lastb and k == len(terms) - 1))
            return mm

        with pe.Fori(0, passes) as i:
            pe.wait_ge(s_t, i * 2 * N + 1)
            unit(i, 0)
            pe.wait_ge(s_oe, i * N + 1)
            unit(i, 1, (0, 1))
            pe.wait_ge(s_ptlo, i * GROUPS + 1)
            pe.wait_ge(s_phi, 9 * i + 3)
            row_group(i, 0, v_col, range(0, 4))
            row_group(i, 1, v_col, range(4, 8))
            unit(i, 1, (2,))
            pe.wait_ge(s_cache, 32 * i + 32)
            row_group(i, 2, v_col, [QT], kc_nat if A else None)
            if not A:
                unit(i, 2, (0, 1))
                pe.wait_ge(s_phi, 9 * i + 6)
                row_group(i, 3, k_col, range(0, 4))
                row_group(i, 4, k_col, range(4, 8))
                pe.wait_ge(s_plo, LOS * i + 2)
                unit(i, 2, (2,))
                row_group(i, 5, k_col, [QT], kc_nat)
            pe.wait_ge(s_plo, LOS * i + 5)
            for s in range(N + 2):
                if s == 2:
                    pe.wait_ge(s_plo, LOS * i + 6)
                    pe.wait_ge(s_nlo, (ROWGROUPS + 1) * i + ROWGROUPS + 1 + 1)
                if A and s == QT + 1:
                    pe.wait_ge(s_t, i * 2 * N + 2 * s + 1)
                    unit(i, 2)
                    pe.wait_ge(s_plo, LOS * i + 9)
                n = len(groups(steps[s - 2][1])) if s >= 2 else 0
                if s < N:
                    logits(i, s, 0)
                if s >= 2:
                    pe.wait_ge(s_norm, i * N + s - 2 + 1)
                for j in range(min(2, n)):
                    turn_over(i, s - 2, j)
                if s < N:
                    logits(i, s, 1)
                if s >= 3:
                    pe.wait_ge(s_oe, i * N + s - 3 + 1 + 1)
                for j in range(n):
                    if j + 2 < n:
                        turn_over(i, s - 2, j + 2)
                    mm = multiply(i, s - 2, j)
                if n:
                    mm.then_inc(s_o, 1)

    def scalar(act):
        def q_piece(i, n, t, u, g2):
            await_piece(c, act, name, i, u, t, s_piece, 3 * i + u)
            nc.scalar.activation(q_hi[:, piece(t)], bank(c, unit_banks[u][t], TP), ACT.Copy,
                                 scale=c.q_scale[:, g2:g2 + 1] if A else 0.125).then_inc(s_phi, 1)

        def exps(i, s, maps):
            g2, t = steps[s]
            L = keys_of(t)
            act.wait_ge(s_nb, i * N + s + 1)
            for m in maps:
                sigma = 2.0 ** (-(2 * g2 + m + 1) / 2) if A else 1.0
                nc.scalar.activation(prob[:, s % 3, m, 0:L], prob[:, s % 3, m, 0:L], ACT.Exp,
                                     bias=stat[:, s % 3, 2 + m:3 + m], scale=sigma,
                                     accum_out=stat[:, s % 3, 4 + m:5 + m]).then_inc(s_exp, 1)

        def transposed(i, s, some):
            t = steps[s][1]
            for j, gr in list(enumerate(groups(t)))[some]:
                n = first_group[s] + j
                act.wait_ge(s_pt, i * GROUPS + n + 1)
                sl, b = n % slots, bank(c, turn_banks[n % 3]).rearrange("p (x w) -> p x w", w=wide)
                if t == SAMPLE:
                    nc.scalar.activation(pt[:, sl, 0, 0], b[:, 0], ACT.Copy).then_inc(s_pthi, 1)
                    nc.scalar.activation(pt[0:NEW, sl, 1, 0], b[0:NEW, 1], ACT.Copy).then_inc(s_pthi, 1)
                else:
                    e = len(gr)
                    nc.scalar.activation(pt[:, sl, 0:e, 0], b[:, 0:e], ACT.Copy).then_inc(s_pthi, 2)

        with act.Fori(0, passes) as i:
            head = act.snap(i * wd)
            act.wait_ge(s_nlo, (ROWGROUPS + 1) * i + 1)
            if A:
                act.dma_start(kc_nat[:, 0:64], columns(c.dram["cache_a_k"], head)).then_inc(s_cache, 16)
                act.dma_start(kc_nat[:, 64:128], columns(c.dram["cache_a_v"], head)).then_inc(s_cache, 16)
            else:
                act.dma_start(kc_nat[:, :], columns(c.dram["cache_b_k"], head)).then_inc(s_cache, 16)
                act.dma_start(vc_nat[:, :], columns(c.dram["cache_b_v"], head)).then_inc(s_cache, 16)
            def rows(n):
                b = bank(c, 4 + n % 2)
                act.wait_ge(s_nt, ROWGROUPS * i + n + 1)
                if n == 0:
                    nc.scalar.activation(v_hi[:, VCACHE, :], vc_nat[:, :], ACT.Copy).then_inc(s_nhi, 1)
                if n == ROWGROUPS - 1:
                    if A:
                        nc.scalar.activation(k_hi[0:64, TOK:KEYCOLS], b[0:64, P:2 * P], ACT.Copy)
                        ins = nc.scalar.activation(k_hi[64:128, TOK:KEYCOLS], b[0:64, P:2 * P], ACT.Copy)
                    else:
                        ins = nc.scalar.activation(k_hi[:, TOK:KEYCOLS], b[:, P:2 * P], ACT.Copy)
                if n < 2:
                    ins = nc.scalar.activation(v_hi[:, 4 * n:4 * n + 4, :], b.rearrange("p (t d) -> p t d", t=4), ACT.Copy)
                elif n == 2:
                    ins = nc.scalar.activation(v_hi[0:NEW, VNEW, :], b[0:NEW, 0:P], ACT.Copy)
                if n < 3 or n == ROWGROUPS - 1:
                    ins.then_inc(s_nhi, 1)

            def k_piece(t):
                await_piece(c, act, name, i, 1, t, s_piece, 3 * i + 1)
                nc.scalar.activation(k_col[:, piece(t)], bank(c, unit_banks[1][t], TP), ACT.Copy)
                nc.scalar.activation(k_hi[:, piece(t)], bank(c, unit_banks[1][t], TP), ACT.Copy).then_inc(s_phi, 1)

            for t in range(PIECES):
                await_piece(c, act, name, i, 0, t, s_piece, 3 * i)
                b = unit_banks[0][t]
                ins = nc.scalar.activation(v_col[:, piece(t)], bank(c, b, TP), ACT.Copy)
                if A:
                    src = c.psum[0:64, 512 * b:512 * b + TP]
                    nc.scalar.activation(k_hi[0:64, piece(t)], src, ACT.Copy)
                    ins = nc.scalar.activation(k_hi[64:128, piece(t)], src, ACT.Copy)
                ins.then_inc(s_phi, 1)
            second = (lambda t: q_piece(i, 3 + t, t, 1, 0)) if A else k_piece
            second(0)
            second(1)
            act.wait_ge(s_cache, 32 * i + 32)
            rows(0)
            rows(1)
            second(2)
            rows(2)
            if not A:
                q_piece(i, 6, 0, 2, 0)
                q_piece(i, 7, 1, 2, 0)
                rows(3)
                rows(4)
                q_piece(i, 8, 2, 2, 0)
                rows(5)
            act.wait_ge(s_nlo, (ROWGROUPS + 1) * i + ROWGROUPS + 2)
            if A:
                outs = [(c.dram["new_a_k_prompt"], c.dram["new_a_k_sample"], k_nat, 0), (c.dram["new_a_v_prompt"], c.dram["new_a_v_sample"], k_nat, 64)]
            else:
                outs = [(c.dram["new_b_k_prompt"], c.dram["new_b_k_sample"], k_nat, 0), (c.dram["new_b_v_prompt"], c.dram["new_b_v_sample"], v_nat, 0)]
            for big, small, rows, o in outs:
                act.dma_start(big[0, 0].rearrange("(t p) h d -> p t (h d)", p=P)[:, :, bass.ds(head, wd)],
                             rows[:, 0:QT, o:o + wd]).then_inc(s_out, 16)
                act.dma_start(columns(small, head),
                             rows[0:NEW, QT, o:o + wd]).then_inc(s_out, 16)
            for s in range(N + 2):
                if A and s == QT + 1:
                    for t in range(PIECES):
                        q_piece(i, 6 + t, t, 2, 1)
                if 1 <= s <= N:
                    exps(i, s - 1, (0, 1) if A else (0,))
                if s >= 2:
                    transposed(i, s - 2, slice(0, 2))
                if 1 <= s <= N and not A:
                    exps(i, s - 1, (1,))
                if s >= 2:
                    transposed(i, s - 2, slice(2, None))

    HI_ROWS = 4 if A else 5

    def vector(v):
        def q_piece(i, n, t, u, g2):
            v.wait_ge(s_phi, 9 * i + n + 1)
            nc.vector.scalar_tensor_tensor(out=q_lo[:, piece(t)], in0=bank(c, unit_banks[u][t], TP),
                                           scalar=c.q_scale[:, g2:g2 + 1] if A else 0.125,
                                           in1=q_hi[:, piece(t)].bitcast(F32), op0=ALU.mult,
                                           op1=ALU.subtract).then_inc(s_plo, 1)

        def read_logits(i, s, m):
            g2, t = steps[s]
            L, sl = keys_of(t), s % 3
            v.wait_ge(s_s, i * 2 * N + 2 * s + m + 1)
            if s == 2 and m == 0:
                v.wait_ge(s_out, 64 * i + 64)
            if A:
                b = c.bias[:, bias_at(t):bias_at(t) + L]
            else:
                o = P * (QT - 1 - t) if t < QT else SEQ
                b = dist[:, o:o + L]
            nc.vector.memset(stat[:, sl, 8 + m:9 + m], 0.0).then_inc(s_cleared, 1)
            nc.vector.tensor_tensor_reduce(prob[:, sl, m, 0:L], c.psum[:, 1024 * m:1024 * m + L], b, 1.0,
                                           LOWEST, ALU.subtract, ALU.max,
                                           stat[:, sl, m:m + 1]).then_inc(s_t, 1)
            if m == 0:
                return
            v.wait_ge(s_t, i * 2 * N + 2 * s + 2 + 1)
            neg = c.neg_sigma[:, g2, :] if A else c.neg_one[:, :]
            nc.vector.tensor_tensor(stat[:, sl, 2:4], stat[:, sl, 0:2], neg, ALU.mult).then_inc(s_nb, 1)

        def normalise(i, s):
            g2, t = steps[s]
            L, sl = keys_of(t), s % 3
            v.wait_ge(s_exp, i * 2 * N + 2 * s + 2)
            nc.vector.reciprocal(stat[:, sl, 6:8], stat[:, sl, 4:6]).then_inc(s_small, 1)
            v.wait_ge(s_small, (i * N + s) * (1 if A else 3) + 1)
            p0, p1 = prob[:, sl, 0, 0:L], prob[:, sl, 1, 0:L]
            if A:
                nc.vector.tensor_scalar(p0, p0, stat[:, sl, 6:7], None, ALU.mult)
                nc.vector.tensor_scalar(p1, p1, stat[:, sl, 7:8], None, ALU.mult).then_inc(s_norm, 1)
            else:
                nc.vector.tensor_tensor(stat[:, sl, 7:8], stat[:, sl, 7:8], c.neg_lam[:, :], ALU.mult).then_inc(s_small, 1)
                v.wait_ge(s_small, (i * N + s) * 3 + 2)
                nc.vector.tensor_scalar(p1, p1, stat[:, sl, 7:8], None, ALU.mult).then_inc(s_small, 1)
                v.wait_ge(s_small, (i * N + s) * 3 + 3)
                nc.vector.scalar_tensor_tensor(out=p0, in0=p0, scalar=stat[:, sl, 6:7], in1=p1, op0=ALU.mult,
                                               op1=ALU.add).then_inc(s_norm, 1)

        def transposed(i, s, some):
            t = steps[s][1]
            for j, gr in list(enumerate(groups(t)))[some]:
                n = first_group[s] + j
                v.wait_ge(s_pthi, 2 * (i * GROUPS + n + 1))
                sl, b = n % slots, bank(c, turn_banks[n % 3]).rearrange("p (x w) -> p x w", w=wide)
                if t == SAMPLE:
                    nc.vector.tensor_tensor(pt[:, sl, 0, 1], b[:, 0], pt[:, sl, 0, 0].bitcast(F32), ALU.subtract)
                    nc.vector.tensor_tensor(pt[0:NEW, sl, 1, 1], b[0:NEW, 1], pt[0:NEW, sl, 1, 0].bitcast(F32),
                                            ALU.subtract).then_inc(s_ptlo, 1)
                else:
                    e = len(gr)
                    nc.vector.tensor_tensor(pt[:, sl, 0:e, 1], b[:, 0:e], pt[:, sl, 0:e, 0].bitcast(F32),
                                            ALU.subtract).then_inc(s_ptlo, 1)

        def take_output(i, s):
            g2, t = steps[s]
            v.wait_ge(s_o, i * N + s + 1)
            q, w_ = (P * t, P) if t < QT else (SEQ, NEW)
            ob = 512 * 6
            if A:
                for m in (0, 1):
                    e = ob + P * m + P
                    ins = nc.vector.tensor_copy(c.o_col[64 * m:64 * m + 64, bass.ds(2 * i + g2, 1), q:q + w_],
                                                c.psum[64:128, e - w_:e].rearrange("p (a t) -> p a t", a=1))
            else:
                o = c.o_col[:, bass.ds(i, 1), q:q + w_]
                hi, lo = (c.psum[:, e - w_:e].rearrange("p (a t) -> p a t", a=1) for e in (ob + P, ob + 2 * P))
                nc.vector.tensor_copy(o, hi).then_inc(s_first, 1)
                v.wait_ge(s_first, i * N + s + 1)
                ins = nc.vector.tensor_tensor(o, lo, o, ALU.add)
            ins.then_inc(s_oe, 1)

        v.sem_inc(s_t, 1)
        v.sem_inc(s_ptlo, 1)
        v.sem_inc(s_oe, 1)
        v.sem_inc(s_nlo, 1)
        if not A:
            v.wait_ge(s_iota, 2)
            nc.vector.scalar_tensor_tensor(out=dist[:, :], in0=dist[:, :], scalar=-1.0, in1=dist[:, :],
                                           op0=ALU.mult, op1=ALU.max).then_inc(s_dist, 1)
            v.wait_ge(s_dist, 1)
            nc.vector.memset(dist[0:64, SEQ - CHUNK:SEQ], BIG).then_inc(s_dist, 1)
            v.wait_ge(s_dist, 2)
            nc.vector.tensor_scalar(dist[:, :], dist[:, :], 0.5, None, ALU.mult).then_inc(s_dist, 1)
            v.wait_ge(s_dist, 3)
        with v.Fori(0, passes) as i:
            def rows_of(n):
                b = bank(c, 4 + n % 2)
                if n == 0:
                    v.wait_ge(s_nhi, HI_ROWS * i + 1)
                    nc.vector.tensor_tensor(v_lo[:, VCACHE, :], vc_nat[:, :], v_hi[:, VCACHE, :].bitcast(F32),
                                            ALU.subtract).then_inc(s_nlo, 1)
                r = n % 3
                rows = k_nat if A or n >= 3 else v_nat
                if n < 3 or n == ROWGROUPS - 1:
                    v.wait_ge(s_nhi, HI_ROWS * i + (n + 2 if n < 3 else 5))
                else:
                    v.wait_ge(s_nt, ROWGROUPS * i + n + 1)
                if n == ROWGROUPS - 1:
                    if A:
                        for m in (0, 1):
                            nc.vector.tensor_tensor(k_lo[64 * m:64 * m + 64, TOK:KEYCOLS], b[0:64, P:2 * P],
                                                    k_hi[0:64, TOK:KEYCOLS].bitcast(F32), ALU.subtract)
                    else:
                        nc.vector.tensor_tensor(k_lo[:, TOK:KEYCOLS], b[:, P:2 * P],
                                                k_hi[:, TOK:KEYCOLS].bitcast(F32), ALU.subtract)
                if n < 2:
                    nc.vector.tensor_tensor(v_lo[:, 4 * r:4 * r + 4, :], b.rearrange("p (t d) -> p t d", t=4),
                                            v_hi[:, 4 * r:4 * r + 4, :].bitcast(F32), ALU.subtract)
                elif n == 2:
                    nc.vector.tensor_tensor(v_lo[0:NEW, VNEW, :], b[0:NEW, 0:P],
                                            v_hi[0:NEW, VNEW, :].bitcast(F32), ALU.subtract)
                if r < 2:
                    nc.vector.tensor_copy(rows[:, 4 * r:4 * r + 4, :], b.rearrange("p (t d) -> p t d", t=4)).then_inc(s_nlo, 1)
                else:
                    nc.vector.tensor_copy(rows[0:NEW, QT, :], b[0:NEW, 0:P]).then_inc(s_nlo, 1)

            def k_piece(t):
                v.wait_ge(s_phi, 9 * i + (0 if A else 3) + t + 1)
                if A:
                    b = unit_banks[0][t]
                    src = c.psum[0:64, 512 * b:512 * b + TP]
                    nc.vector.tensor_tensor(k_lo[0:64, piece(t)], src, k_hi[0:64, piece(t)].bitcast(F32), ALU.subtract)
                    ins = nc.vector.tensor_tensor(k_lo[64:128, piece(t)], src, k_hi[0:64, piece(t)].bitcast(F32),
                                                  ALU.subtract)
                else:
                    ins = nc.vector.tensor_tensor(k_lo[:, piece(t)], bank(c, unit_banks[1][t], TP),
                                                  k_hi[:, piece(t)].bitcast(F32), ALU.subtract)
                ins.then_inc(s_plo, 1)

            if A:
                for t in range(PIECES):
                    k_piece(t)
            second = (lambda t: q_piece(i, 3 + t, t, 1, 0)) if A else k_piece
            second(0)
            second(1)
            rows_of(0)
            rows_of(1)
            second(2)
            rows_of(2)
            if not A:
                q_piece(i, 6, 0, 2, 0)
                q_piece(i, 7, 1, 2, 0)
                rows_of(3)
                rows_of(4)
                q_piece(i, 8, 2, 2, 0)
                rows_of(5)
            for s in range(N + 3):
                if A and s == QT + 1:
                    for t in range(PIECES):
                        q_piece(i, 6 + t, t, 2, 1)
                if s >= 3:
                    take_output(i, s - 3)
                if s < N:
                    read_logits(i, s, 0)
                if 2 <= s < N + 2:
                    transposed(i, s - 2, slice(0, 2))
                if s < N:
                    read_logits(i, s, 1)
                if 2 <= s < N + 2:
                    transposed(i, s - 2, slice(2, 3))
                if 1 <= s <= N:
                    normalise(i, s - 1)
                if 2 <= s < N + 2:
                    transposed(i, s - 2, slice(3, None))
            if A:
                nc.vector.tensor_scalar(c.bias[:, :], c.bias[:, :], 0.25, None, ALU.mult).then_inc(s_dist, 1)
                v.wait_ge(s_dist, i + 1)
            else:
                nc.vector.tensor_scalar(dist[:, :], dist[:, :], 0.5, None, ALU.mult).then_inc(s_dist, 1)
                v.wait_ge(s_dist, i + 4)

    return sync, pool, tensor, scalar, vector


def out_projection(c, kind):
    nc = c.nc
    name = "out" + kind
    o_hi = c.at("o_hi" + kind, [P, KC, TOK], F32R, 0)
    o_lo = c.at("o_lo" + kind, [P, KC, TOK], F32R, 33792)
    if kind == "B":
        sq = c.at("o_sq", [P, PIECES, KC, TP], F32, 33792)
        root = c.at("o_root", [P, PIECES, TP], F32, 67584)
        pick = c.at("o_pick", [P, 2 * BH - 1], F32, 67584 + 4 * TOK)
    S = lambda n: c.sem(n + kind)
    s_hi, s_lo, s_p, s_y = S("o_hi_done"), S("o_lo_done"), S("out_pieces"), S("out_added")
    if kind == "B":
        s_sq, s_ms, s_sd, s_rs = S("o_squares"), S("o_mean_sq"), S("o_rooted"), S("o_scaled")
        s_pick, s_rec, s_bc = S("o_picker"), S("o_reciprocal"), S("o_spread")
    w = (c.dram["a_w_out"] if kind == "A" else c.dram["b_w_out"])[0].rearrange("(k p) n -> p k n", p=P)

    def sync(sp):
        with sp.Fori(0, 4) as i:
            for u in (0, 1):
                load_unit(c, sp, name, i, u, [(whole, w[:, :, bass.ds(2 * P * i + P * u, P)])], KC)

    def pool(g):
        with g.Fori(0, 4) as i:
            for u in (0, 1):
                split_unit(c, g, name, i, u, KC)

    def tensor(pe):
        if kind == "B":
            for t in range(PIECES):
                pe.wait_ge(s_sq, t + 1)
                pe.wait_ge(s_pick, 2)
                for h in range(BH):
                    mm = nc.tensor.matmul(c.psum[0:BH, 512 * t:512 * t + TP], pick[:, BH - 1 - h:2 * BH - 1 - h],
                                          sq[:, t, h, :], start=(h == 0), stop=(h == BH - 1))
                mm.then_inc(s_ms, 1)
            for t in range(PIECES):
                pe.wait_ge(s_rec, t + 1)
                for h in range(BH):
                    n = BH * t + h
                    if n >= 5:
                        pe.wait_ge(s_rs, n - 4)
                    nc.tensor.matmul(bank(c, 3 + n % 5, TP), c.ident[0:BH, h:h + 1].to_broadcast([BH, P]),
                                     root[0:BH, t, :], start=True, stop=True).then_inc(s_bc, 1)
            pe.wait_ge(s_rs, 3 * BH)
        with pe.Fori(0, 4) as i:
            for u in (0, 1):
                s = unit_ready(c, pe, name, i, u)
                for t in range(PIECES):
                    pe.wait_ge(s_lo, t + 1)
                    pe.wait_ge(s_y, 6 * i + 3 * u + t + 1)
                    last = unit_product(c, bank(c, 3 * u + t, TP), s, KC, o_hi, o_lo, t)
                    piece_done(c, last, t, s_p, s)

    def scalar(act):
        if kind == "B":
            for t in range(PIECES):
                nc.scalar.activation(sq[:, t], c.o_col[:, :, piece(t)], ACT.Square).then_inc(s_sq, 1)
            for t in range(PIECES):
                act.wait_ge(s_ms, t + 1)
                nc.scalar.activation(root[0:BH, t, :], c.psum[0:BH, 512 * t:512 * t + TP], ACT.Sqrt,
                                     bias=c.eps[0:BH, :]).then_inc(s_sd, 1)
        for t in range(PIECES):
            if kind == "B":
                act.wait_ge(s_rs, BH * (t + 1))
            nc.scalar.activation(o_hi[:, :, piece(t)], c.o_col[:, :, piece(t)], ACT.Copy).then_inc(s_hi, 1)

    def vector(v):
        if kind == "B":
            nc.vector.memset(pick[:, :], 0.0).then_inc(s_pick, 1)
            v.wait_ge(s_pick, 1)
            nc.vector.memset(pick[:, BH - 1:BH], 1.0 / P).then_inc(s_pick, 1)
            for t in range(PIECES):
                v.wait_ge(s_sd, t + 1)
                nc.vector.reciprocal(root[0:BH, t, :], root[0:BH, t, :]).then_inc(s_rec, 1)
            for t in range(PIECES):
                for h in range(BH):
                    n = BH * t + h
                    v.wait_ge(s_bc, n + 1)
                    o = c.o_col[:, h, piece(t)]
                    nc.vector.scalar_tensor_tensor(out=o, in0=o, scalar=c.rms_gain[:, :], in1=bank(c, 3 + n % 5, TP),
                                                   op0=ALU.mult, op1=ALU.mult).then_inc(s_rs, 1)
            v.wait_ge(s_ms, 3)
        for t in range(PIECES):
            v.wait_ge(s_hi, t + 1)
            nc.vector.tensor_tensor(o_lo[:, :, piece(t)], c.o_col[:, :, piece(t)], o_hi[:, :, piece(t)].bitcast(F32),
                                    ALU.subtract).then_inc(s_lo, 1)
        v.wait_ge(s_lo, 3)
        v.sem_inc(s_y, 6)
        with v.Fori(0, 4) as i:
            for u in (0, 1):
                for t in range(PIECES):
                    n = 6 * i + 3 * u + t
                    y = c.o_col[:, bass.ds(2 * i + u, 1), piece(t)]
                    b = bank(c, 3 * u + t, TP).rearrange("p (a t) -> p a t", a=1)
                    await_piece(c, v, name, i, u, t, s_p, 2 * i + u)
                    nc.vector.scalar_tensor_tensor(out=y, in0=c.x_hi[:, bass.ds(2 * i + u, 1), piece(t)].bitcast(F32),
                                                   scalar=ALPHA, in1=b, op0=ALU.mult, op1=ALU.add).then_inc(s_y, 1)
                    v.wait_ge(s_y, n + 7)
                    nc.vector.scalar_tensor_tensor(out=y, in0=c.x_lo[:, bass.ds(2 * i + u, 1), piece(t)].bitcast(F32),
                                                   scalar=ALPHA, in1=y, op0=ALU.mult, op1=ALU.add)

    return sync, pool, tensor, scalar, vector


def layer_norm(c, layer, which):
    nc = c.nc
    tag = f"_{layer}{which}"
    sq = [c.at(f"ln_sq{j}{tag}", [P, KC, TP], F32, 11264 * j) for j in (0, 1)]
    sd = c.at("ln_sd" + tag, [P, PIECES, TP], F32, 22528)
    names = ("ln_mean", "ln_centred", "ln_squares", "ln_var", "ln_root", "ln_steps", "ln_full", "ln_hi", "ln_lo")
    if not c.ln_sems:
        c.ln_sems = [c.sem(n) for n in names]
    s_mean, s_d, s_sq, s_var, s_sd, s_r, s_full, s_hi, s_lo = c.ln_sems
    done = PIECES * (2 * layer + which)
    last_one = (layer, which) == (DEPTH - 1, 1)
    par = lambda kind, k: c.params[:, 32 * kind + 16 * layer + 8 * which + k:32 * kind + 16 * layer + 8 * which + k + 1]

    def pool(g):
        if last_one:
            return
        for t in range(PIECES - 1):
            g.wait_ge(s_full, KC * (done + t + 1))
            g.wait_ge(s_hi, KC * (done + t + 1))
            nc.gpsimd.tensor_tensor(c.x_lo[:, :, piece(t)], c.o_col[:, :, piece(t)],
                                    c.x_hi[:, :, piece(t)].bitcast(F32), ALU.subtract).then_inc(s_lo, 1)

    def tensor(pe):
        for t in range(PIECES):
            for k in range(KC):
                mm = nc.tensor.matmul(bank(c, t, TP), c.mean_d[:, :], c.o_col[:, k, piece(t)],
                                      start=(k == 0), stop=(k == KC - 1))
            mm.then_inc(s_mean, 1)
        for t in range(PIECES):
            pe.wait_ge(s_sq, done + t + 1)
            for k in range(KC):
                mm = nc.tensor.matmul(bank(c, 3 + t, TP), c.mean_d[:, :], sq[t % 2][:, k, :],
                                      start=(k == 0), stop=(k == KC - 1))
            mm.then_inc(s_var, 1)

    def scalar(act):
        for t in range(PIECES):
            act.wait_ge(s_d, done + t + 1)
            if t >= 2:
                act.wait_ge(s_var, done + t - 1)
            nc.scalar.activation(sq[t % 2][:, :, :], c.o_col[:, :, piece(t)], ACT.Square).then_inc(s_sq, 1)
        for t in range(PIECES):
            act.wait_ge(s_var, done + t + 1)
            nc.scalar.activation(sd[:, t, :], bank(c, 3 + t, TP), ACT.Sqrt, bias=c.eps[:, :]).then_inc(s_sd, 1)
        for t in range(PIECES):
            act.wait_ge(s_r, 2 * (done + t) + 2)
            if not last_one:
                for k in range(KC):
                    nc.scalar.activation(c.x_hi[:, k, piece(t)], c.o_col[:, k, piece(t)], ACT.Identity,
                                         bias=par(1, k), scale=par(0, k)).then_inc(s_hi, 1)

    def vector(v):
        for t in range(PIECES):
            v.wait_ge(s_mean, done + t + 1)
            o = c.o_col[:, :, piece(t)]
            mean = bank(c, t, TP).rearrange("p (a t) -> p a t", a=1).to_broadcast([P, KC, TP])
            nc.vector.tensor_tensor(o, o, mean, ALU.subtract).then_inc(s_d, 1)
        def scale(t):
            o = c.o_col[:, :, piece(t)]
            v.wait_ge(s_sd, done + t + 1)
            nc.vector.reciprocal(sd[:, t, :], sd[:, t, :]).then_inc(s_r, 1)
            v.wait_ge(s_r, 2 * (done + t) + 1)
            r = sd[:, t:t + 1, :].to_broadcast([P, KC, TP])
            nc.vector.tensor_tensor(o, o, r, ALU.mult).then_inc(s_r, 1)

        def finish(t):
            v.wait_ge(s_r, 2 * (done + t) + 2)
            for k in range(KC):
                if not last_one:
                    v.wait_ge(s_hi, KC * (done + t) + k + 1)
                nc.vector.tensor_scalar(c.o_col[:, k, piece(t)], c.o_col[:, k, piece(t)], par(0, k), par(1, k),
                                        ALU.mult, ALU.add).then_inc(s_full, 1)

        scale(0)
        for t in range(PIECES):
            if t + 1 < PIECES:
                scale(t + 1)
            finish(t)
        if not last_one:
            v.wait_ge(s_full, KC * (done + PIECES))
            nc.vector.tensor_tensor(c.x_lo[:, :, piece(PIECES - 1)], c.o_col[:, :, piece(PIECES - 1)],
                                    c.x_hi[:, :, piece(PIECES - 1)].bitcast(F32), ALU.subtract).then_inc(s_lo, 1)

    def ready(eng):
        if not last_one:
            eng.wait_ge(s_lo, done + PIECES)
    return None, pool, tensor, scalar, vector, ready


def ffn(c, layer):
    nc = c.nc
    tag = str(layer)
    p_nat = c.at("p_nat" + tag, [P, QT + 1, PLE], F32, 0)
    p_hi, p_lo = c.at("p_hi" + tag, [P, 2, TOK], F32R, 9216), c.at("p_lo" + tag, [P, 2, TOK], F32R, 17664)
    h_hi, h_lo = c.at("h_hi" + tag, [P, 2, TOK], F32R, 26112), c.at("h_lo" + tag, [P, 2, TOK], F32R, 34560)
    gate = c.at("gate" + tag, [P, 2, TOK], F32, 43008)
    S = lambda n: c.sem(n + tag)
    s_pn, s_pt, s_ph, s_pl = S("p_loaded"), S("p_transposed"), S("p_hi_done"), S("p_lo_done")
    s_gp, s_sg, s_pp, s_t, s_acc = S("gate_pieces"), S("gate_done"), S("ple_pieces"), S("gated"), S("ple_added")
    s_g, s_si, s_u, s_h, s_hh, s_hl = S("ffn_gate"), S("silu_done"), S("ffn_up"), S("h_done"), S("h_hi_done"), S("h_lo_done")
    s_d, s_da = S("down_pieces"), S("down_added")
    wg = c.dram["ple_w_gate"][layer].rearrange("(k p) n -> p k n", p=P)
    wp = c.dram["ple_w_proj"][layer].rearrange("(k p) n -> p k n", p=P)
    w13 = c.dram["ffn_w13"][layer].rearrange("(k p) n -> p k n", p=P)
    w2 = c.dram["ffn_w2"][layer]
    ple, fn = "ple" + tag, "ffn" + tag
    PAIRS = DFF // P // 2
    no = c.phase_no

    def sync(sp):
        sp.wait_ge(c.phase_over, 3 * no)
        sp.dma_start(p_nat[:, 0:QT, :], c.dram["p_prompt"][layer, 0].rearrange("(t p) n -> p t n", p=P)).then_inc(s_pn, 16)
        sp.dma_start(p_nat[0:NEW, QT, :], c.dram["p_sample"][layer, 0]).then_inc(s_pn, 16)
        with sp.Fori(0, KC // 2) as i:
            for j in (0, 1):
                load_unit(c, sp, ple, i, 2 * j, [(whole, wg[:, :, bass.ds(2 * P * i + P * j, P)])], KC)
                load_unit(c, sp, ple, i, 2 * j + 1, [(whole, wp[:, :, bass.ds(2 * P * i + P * j, P)])], 2)
        with sp.Fori(0, PAIRS) as i:
            for j in (0, 1):
                load_unit(c, sp, fn, i, 2 * j, [(whole, w13[:, :, bass.ds(2 * P * i + P * j, P)])], KC)
                load_unit(c, sp, fn, i, 2 * j + 1, [(whole, w13[:, :, bass.ds(DFF + 2 * P * i + P * j, P)])], KC)
            for j in (0, 1):
                load_unit(c, sp, fn, i, 4 + j, [(lambda x: x.rearrange("p k n -> p (k n)"),
                                                 w2[bass.ds(2 * P * i + P * j, P), :])], KC)

    def pool(g):
        with g.Fori(0, KC // 2) as i:
            for j in (0, 1):
                split_unit(c, g, ple, i, 2 * j, KC)
                split_unit(c, g, ple, i, 2 * j + 1, 2)
        with g.Fori(0, PAIRS) as i:
            for u in range(6):
                split_unit(c, g, fn, i, u, KC)

    def tensor(pe):
        pe.wait_ge(s_pn, 32)
        for k in (0, 1):
            for b in (0, 1):
                for j in range(4):
                    mm = nc.tensor.transpose(bank(c, 2 * k + b)[:, P * j:P * j + P],
                                             p_nat[:, 4 * b + j, P * k:P * k + P], c.ident[:, :])
                mm.then_inc(s_pt, 1)
        for k in (0, 1):
            mm = nc.tensor.transpose(bank(c, 4)[:, NEW * k:NEW * k + NEW], p_nat[0:NEW, QT, P * k:P * k + P],
                                     c.ident[0:NEW, 0:NEW])
        mm.then_inc(s_pt, 1)
        pe.wait_ge(s_pl, 5)
        with pe.Fori(0, KC // 2) as i:
            for j in (0, 1):
                s = unit_ready(c, pe, ple, i, 2 * j)
                for t in range(PIECES):
                    pe.wait_ge(s_sg, 6 * i + 3 * j + t + 1)
                    last = unit_product(c, bank(c, t, TP), s, KC, c.x_hi, c.x_lo, t)
                    piece_done(c, last, t, s_gp, s)
                s = unit_ready(c, pe, ple, i, 2 * j + 1)
                for t in range(PIECES):
                    pe.wait_ge(s_t, 6 * i + 3 * j + t + 1)
                    last = unit_product(c, bank(c, 3 + t, TP), s, 2, p_hi, p_lo, t)
                    piece_done(c, last, t, s_pp, s)
        pe.wait_ge(s_t, 3 * KC + 3)
        with pe.Fori(0, PAIRS) as i:
            for j in (0, 1):
                s = unit_ready(c, pe, fn, i, 2 * j)
                for t in range(PIECES):
                    if j == 0:
                        pe.wait_ge(s_da, 24 * i + 19 + t)
                    pe.wait_ge(s_si, 6 * i + 3 * j + t + 1)
                    last = unit_product(c, bank(c, t, TP), s, KC, c.x_hi, c.x_lo, t)
                    piece_done(c, last, t, s_g, s)
                s = unit_ready(c, pe, fn, i, 2 * j + 1)
                for t in range(PIECES):
                    if j == 0:
                        pe.wait_ge(s_da, 24 * i + 22 + t)
                    pe.wait_ge(s_h, 6 * i + 3 * j + t + 1)
                    last = unit_product(c, bank(c, 3 + t, TP), s, KC, c.x_hi, c.x_lo, t)
                    piece_done(c, last, t, s_u, s)
            unit_ready(c, pe, fn, i, 4)
            unit_ready(c, pe, fn, i, 5)
            for t in range(PIECES):
                pe.wait_ge(s_hl, 6 * i + 3 + t + 1 + 3)
                for m in range(KC):
                    b = (6 + m) % 8
                    n = KC * t + m
                    if t > 0:
                        pe.wait_ge(s_da, 24 * i + 24 + n - 8 + 1)
                    elif b < 3:
                        pe.wait_ge(s_si, 6 * i + 3 + b + 1 + 3)
                    elif b < 6:
                        pe.wait_ge(s_h, 6 * i + 3 + (b - 3) + 1 + 3)
                    o, at_end = bank(c, b, TP), n == 3 * KC - 1
                    for j in (0, 1):
                        s = turn(fn, i, 4 + j)[0]
                        for k, (w, h) in enumerate(((c.w_hi, h_hi), (c.w_hi, h_lo), (c.w_lo, h_hi))):
                            mm = nc.tensor.matmul(o, w[s][:, m, :], h[:, j, piece(t)],
                                                  start=(j == 0 and k == 0), stop=(j == 1 and k == 2))
                        if at_end:
                            mm.then_inc(c.used[s], 1)
                    if not at_end:
                        mm.then_inc(s_d, 1)

    def scalar(act):
        for k in (0, 1):
            for b in (0, 1):
                act.wait_ge(s_pt, 2 * k + b + 1)
                nc.scalar.activation(p_hi[:, k, 512 * b:512 * b + 512], bank(c, 2 * k + b), ACT.Copy).then_inc(s_ph, 1)
        act.wait_ge(s_pt, 5)
        nc.scalar.activation(p_hi[:, :, SEQ:TOK], bank(c, 4, 2 * NEW).rearrange("p (k t) -> p k t", k=2), ACT.Copy).then_inc(s_ph, 1)
        act.sem_inc(s_sg, 3)
        act.sem_inc(s_si, 3)
        with act.Fori(0, KC // 2) as i:
            for j in (0, 1):
                for t in range(PIECES):
                    await_piece(c, act, ple, i, 2 * j, t, s_gp, 2 * i + j)
                    act.wait_ge(s_acc, 6 * i + 3 * j + t + 1)
                    nc.scalar.activation(gate[:, 0, piece(t)], bank(c, t, TP), ACT.Sigmoid).then_inc(s_sg, 1)
        act.wait_ge(s_acc, 3 * KC + 3)
        with act.Fori(0, PAIRS) as i:
            for j in (0, 1):
                for t in range(PIECES):
                    n = 6 * i + 3 * j + t
                    await_piece(c, act, fn, i, 2 * j, t, s_g, 2 * i + j)
                    act.wait_ge(s_hl, n + 1)
                    nc.scalar.activation(gate[:, 0, piece(t)], bank(c, t, TP), ACT.Silu).then_inc(s_si, 1)
                for t in range(PIECES):
                    act.wait_ge(s_h, 6 * i + 3 * j + t + 1 + 3)
                    nc.scalar.activation(h_hi[:, j, piece(t)], gate[:, 1, piece(t)], ACT.Copy).then_inc(s_hh, 1)

    def vector(v):
        for k in (0, 1):
            for b in (0, 1):
                v.wait_ge(s_ph, 2 * k + b + 1)
                nc.vector.tensor_tensor(p_lo[:, k, 512 * b:512 * b + 512], bank(c, 2 * k + b),
                                        p_hi[:, k, 512 * b:512 * b + 512].bitcast(F32), ALU.subtract).then_inc(s_pl, 1)
        v.wait_ge(s_ph, 5)
        nc.vector.tensor_tensor(p_lo[:, :, SEQ:TOK], bank(c, 4, 2 * NEW).rearrange("p (k t) -> p k t", k=2),
                                p_hi[:, :, SEQ:TOK].bitcast(F32), ALU.subtract).then_inc(s_pl, 1)
        v.sem_inc(s_t, 3)
        v.sem_inc(s_acc, 3)
        v.sem_inc(s_h, 3)
        v.sem_inc(s_hl, 3)
        v.sem_inc(s_da, 24)
        with v.Fori(0, KC // 2) as i:
            for j in (0, 1):
                for t in range(PIECES):
                    n = 6 * i + 3 * j + t
                    await_piece(c, v, ple, i, 2 * j + 1, t, s_pp, 2 * i + j)
                    v.wait_ge(s_sg, n + 1 + 3)
                    g = gate[:, 0, piece(t)]
                    nc.vector.tensor_tensor(g, bank(c, 3 + t, TP), g, ALU.mult).then_inc(s_t, 1)
                    v.wait_ge(s_t, n + 1 + 3)
                    o = c.o_col[:, bass.ds(2 * i + j, 1), piece(t)]
                    nc.vector.scalar_tensor_tensor(out=o, in0=o, scalar=ALPHA, in1=g.rearrange("p (a t) -> p a t", a=1),
                                                   op0=ALU.mult, op1=ALU.add).then_inc(s_acc, 1)
        with v.Fori(0, PAIRS) as i:
            for j in (0, 1):
                for t in range(PIECES):
                    n = 6 * i + 3 * j + t
                    await_piece(c, v, fn, i, 2 * j + 1, t, s_u, 2 * i + j)
                    v.wait_ge(s_si, n + 1 + 3)
                    v.wait_ge(s_hl, n + 1)
                    nc.vector.tensor_tensor(gate[:, 1, piece(t)], bank(c, 3 + t, TP), gate[:, 0, piece(t)],
                                            ALU.mult).then_inc(s_h, 1)
                for t in range(PIECES):
                    n = 6 * i + 3 * j + t
                    v.wait_ge(s_hh, n + 1)
                    nc.vector.tensor_tensor(h_lo[:, j, piece(t)], gate[:, 1, piece(t)],
                                            h_hi[:, j, piece(t)].bitcast(F32), ALU.subtract).then_inc(s_hl, 1)
            for t in range(PIECES):
                for m in range(KC):
                    if KC * t + m < 3 * KC - 1:
                        v.wait_ge(s_d, (3 * KC - 1) * i + KC * t + m + 1)
                    else:
                        s_, n_ = turn(fn, i, 5)
                        v.wait_ge(c.used[s_], n_ + 2)
                    o = c.o_col[:, m, piece(t)]
                    nc.vector.tensor_tensor(o, bank(c, (6 + m) % 8, TP), o, ALU.add).then_inc(s_da, 1)
        v.wait_ge(s_da, 24 * PAIRS + 24)

    return sync, pool, tensor, scalar, vector


def store_y(c):
    nc = c.nc
    rows = c.at("y_rows", [P, 4, D], F32, 32768)
    s_t, s_c, s_s = c.sem("y_transposed"), c.sem("y_copied"), [c.sem(f"y_stored{j}") for j in range(4)]

    def sync(sp):
        for t in range(QT + 1):
            n = P if t < QT else NEW
            sp.wait_ge(s_c, 2 * t + 2)
            dst = c.dram["y_prompt"][0, P * t:P * t + P, :] if t < QT else c.dram["y_sample"][0]
            sp.dma_start(dst, rows[0:n, t % 4, :]).then_inc(s_s[t % 4], 16)
        for j in range(4):
            sp.wait_ge(s_s[j], 16 * len(range(j, QT + 1, 4)))

    def tensor(pe):
        for t in range(QT + 1):
            n = P if t < QT else NEW
            for b in (0, 1):
                k = 2 * t + b
                if k >= 8:
                    pe.wait_ge(s_c, k - 7)
                for j in range(4):
                    mm = nc.tensor.transpose(bank(c, k % 8)[0:n, P * j:P * j + P],
                                             c.o_col[:, 4 * b + j, P * t:P * t + n], c.ident[:, :])
                mm.then_inc(s_t, 1)

    def scalar(act):
        for t in range(QT + 1):
            n = P if t < QT else NEW
            for b in (0, 1):
                k = 2 * t + b
                act.wait_ge(s_t, k + 1)
                if t >= 4:
                    act.wait_ge(s_s[t % 4], 16 * (t // 4))
                nc.scalar.activation(rows[0:n, t % 4, 512 * b:512 * b + 512], bank(c, k % 8)[0:n, :], ACT.Copy).then_inc(s_c, 1)

    return sync, None, tensor, scalar, None


INS = ['x_prompt', 'x_sample', 'cache_a_k', 'cache_a_v', 'cache_a_kidx', 'cache_b_k', 'cache_b_v',
       'p_prompt', 'p_sample', 'a_w_in', 'a_w_out', 'b_w_in', 'b_lambda', 'b_subln', 'b_w_out',
       'ffn_w13', 'ffn_w2', 'ple_w_proj', 'ple_w_gate', 'ln_gain', 'ln_bias']
OUTS = [('y_prompt', (1, SEQ, D)), ('y_sample', (1, NEW, D)),
        ('new_a_k_prompt', (1, 1, SEQ, KV, 64)), ('new_a_v_prompt', (1, 1, SEQ, KV, 64)),
        ('new_a_kidx_prompt', (1, 1, SEQ, IDXD)),
        ('new_b_k_prompt', (1, 1, SEQ, BH, P)), ('new_b_v_prompt', (1, 1, SEQ, BH, P)),
        ('new_a_k_sample', (1, 1, NEW, KV, 64)), ('new_a_v_sample', (1, 1, NEW, KV, 64)),
        ('new_a_kidx_sample', (1, 1, NEW, IDXD)),
        ('new_b_k_sample', (1, 1, NEW, BH, P)), ('new_b_v_sample', (1, 1, NEW, BH, P))]


def program(nc, drams):
    with ExitStack() as ctx:
        c = Core()
        c.nc = nc
        c.dram = drams
        c.sem = lambda n: ctx.enter_context(nc.semaphore(n))

        def sb(n, shape, dt=F32):
            return ctx.enter_context(nc.sbuf_tensor(n, shape, dt))

        c.x_rows = c.dram["x_prompt"].rearrange("b t d -> (b t) d")
        c.psum = ctx.enter_context(nc.psum_tensor("psum", [P, 8 * 512], F32))
        c.x_hi, c.x_lo = sb("x_hi", [P, KC, TOK], F32R), sb("x_lo", [P, KC, TOK], F32R)
        c.o_col = sb("o_col", [P, KC, TOK])
        c.w_raw = [sb(f"w_raw{s}", [P, KC, P]) for s in (0, 1)]
        c.w_hi = [sb(f"w_hi{s}", [P, KC, P], F32R) for s in (0, 1)]
        c.w_lo = [sb(f"w_lo{s}", [P, KC, P], F32R) for s in (0, 1)]
        c.zeros, c.ident = sb("zeros", [P, 1]), sb("ident", [P, P])
        c.mean_d = sb("mean_d", [P, P])
        c.q_scale, c.neg_sigma, c.neg_one = sb("q_scale", [P, 2]), sb("neg_sigma", [P, 2, 2]), sb("neg_one", [P, 2])
        c.eps, c.neg_lam, c.rms_gain = sb("eps", [P, 1]), sb("neg_lam", [P, 1]), sb("rms_gain", [P, 1])
        c.params, c.idx_w = sb("params", [P, 66]), sb("idx_w", [P, 9, 8])
        c.end = nc.sbuf_usable_end
        c.base = (nc.sbuf_base + 63) // 64 * 64
        arena = sb("arena", [P, (c.end - c.base) // 4 - 16])
        c.at = lambda n, shape, dt, off: nc.alloc_sbuf_tensor_at(n, shape, dt, offset=c.base + off)
        bias_cols = bias_at(QT) + PAST + NEW
        c.bias_bytes = 4 * bias_cols
        for s in (0, 1):
            c.w_raw.append(c.at(f"w_raw{s + 2}", [P, KC, P], F32, 51456 + 4096 * s))
            c.w_hi.append(c.at(f"w_hi{s + 2}", [P, KC, P], F32R, 59648 + 4096 * s))
            c.w_lo.append(c.at(f"w_lo{s + 2}", [P, KC, P], F32R, 67840 + 4096 * s))
        c.bias = c.at("bias", [P, bias_cols], F32, 0)
        c.dist = c.at("dist", [P, SEQ], F32, (c.end - c.base - 4096) // 64 * 64)
        c.loaded, c.split, c.used = ([c.sem(f"{n}{s}") for s in range(4)] for n in ("w_loaded", "w_split", "w_used"))
        c.phase_over = c.sem("phase_over")
        c.phase_no = 0
        c.ln_sems = None
        c.phases = []
        for make, *args in ((load_x,), (index_projection,), (selection,), (attention, "A"), (out_projection, "A"),
                            (layer_norm, 0, 0), (ffn, 0), (layer_norm, 0, 1), (attention, "B"), (out_projection, "B"),
                            (layer_norm, 1, 0), (ffn, 1), (layer_norm, 1, 1), (store_y,))[:LIMIT]:
            c.phase_no = len(c.phases)
            c.phases.append(make(c, *args))

        def compute(eng, which):
            for n, phase in enumerate(c.phases):
                if phase[which]:
                    phase[which](eng)
                eng.drain().then_inc(c.phase_over, 1)
                eng.wait_ge(c.phase_over, 3 * n + 3)
                for also in phase[5:]:
                    also(eng)

        block = ctx.enter_context(nc.Block())

        @block.sync
        def _(sp):
            for phase in c.phases:
                if phase[0]:
                    phase[0](sp)

        @block.gpsimd
        def _(pool):
            for phase in c.phases:
                if phase[1]:
                    phase[1](pool)

        @block.tensor
        def _(pe):
            compute(pe, 2)

        @block.scalar
        def _(act):
            compute(act, 3)

        @block.vector
        def _(dve):
            compute(dve, 4)


def kernel(**inputs):
    import numpy as _np
    import concourse.bacc as _bacc
    from concourse import mybir as _mybir
    from concourse.bass_utils import run_bass_kernel_spmd as _run

    nc = _bacc.Bacc("TRN2", target_bir_lowering=False, num_devices=1)
    arrays, drams = {}, {}
    for name in INS:
        a = _np.ascontiguousarray(inputs[name])
        arrays[f"in_{name}_dram"] = a
        drams[name] = nc.dram_tensor(f"in_{name}_dram", a.shape, _mybir.dt.from_np(a.dtype), kind="ExternalInput").ap()
    for name, shape in OUTS:
        drams[name] = nc.dram_tensor(f"out_{name}_dram", shape, F32, kind="ExternalOutput").ap()
    program(nc, drams)
    r = _run(nc, [arrays], core_ids=[0])
    return tuple(r.results[0][f"out_{name}_dram"] for name, _ in OUTS)
```
